# Optimizing a Trainium2 kernel written in Bass

```python
import jax, jax.numpy as jnp
from jax import lax
import numpy as np

D_MODEL = 1024
BATCH = 1
SEQ = 128
DEPTH = 1
DEC_BATCH = 1
DEC_SEQ = 1024
PAST_LEN = 256

GRID_W = 64
N_RET_HEADS = 8
RET_DK = 64
RET_DV = 128
D_RET_QK = N_RET_HEADS * RET_DK
D_RET_V = N_RET_HEADS * RET_DV
RET_CHUNK = 128
D_CONV = 1024
CONV_W = 3
N_EXPERTS = 16
EC_CAPACITY_FACTOR = 2
EXPERT_FF = 1024
RMS_EPS = 1e-6
GN_EPS = 1e-5
ROPE_BASE = 10000.0
SPLIT_POINTS = (
    D_RET_QK,
    2 * D_RET_QK,
    2 * D_RET_QK + D_RET_V,
    2 * D_RET_QK + 2 * D_RET_V,
    2 * D_RET_QK + 2 * D_RET_V + D_CONV,
    2 * D_RET_QK + 2 * D_RET_V + 2 * D_CONV,
    2 * D_RET_QK + 2 * D_RET_V + 3 * D_CONV,
    2 * D_RET_QK + 2 * D_RET_V + 3 * D_CONV + D_MODEL,
)
D_IN_TOTAL = 2 * D_RET_QK + 2 * D_RET_V + 3 * D_CONV + 2 * D_MODEL

kernel_name = 'hybrid_retention_shortconv_ecmoe_diffusion_step'

def rmsnorm(x, g):
    x32 = x.astype(jnp.float32)
    y = x32 * lax.rsqrt(jnp.mean(x32 * x32, axis=-1, keepdims=True) + RMS_EPS)
    return (y * g.astype(jnp.float32)).astype(x.dtype)

def rot_half(x, ang):
    x1, x2 = jnp.split(x, 2, axis=-1)
    cos, sin = jnp.cos(ang), jnp.sin(ang)
    return jnp.concatenate([x1 * cos - x2 * sin, x1 * sin + x2 * cos], axis=-1)

def rope_2d(x):
    l = x.shape[2]
    rows = l // GRID_W
    r_idx = jnp.broadcast_to(jnp.arange(rows, dtype=jnp.float32)[:, None], (rows, GRID_W)).reshape(-1)
    c_idx = jnp.broadcast_to(jnp.arange(GRID_W, dtype=jnp.float32)[None, :], (rows, GRID_W)).reshape(-1)
    n_freq = RET_DK // 4
    inv = ROPE_BASE ** (-jnp.arange(n_freq, dtype=jnp.float32) / n_freq)
    xr, xc = jnp.split(x.astype(jnp.float32), 2, axis=-1)
    out = jnp.concatenate([rot_half(xr, r_idx[:, None] * inv), rot_half(xc, c_idx[:, None] * inv)], axis=-1)
    return out.astype(x.dtype)

def retention_chunkwise(q, k, v, log_gamma, s0):
    b, h, l, dk = q.shape
    dv = v.shape[-1]
    nc = l // RET_CHUNK
    qc = q.astype(jnp.float32).reshape(b, h, nc, RET_CHUNK, dk)
    kc = k.astype(jnp.float32).reshape(b, h, nc, RET_CHUNK, dk)
    vc = v.astype(jnp.float32).reshape(b, h, nc, RET_CHUNK, dv)
    pos = jnp.arange(RET_CHUNK, dtype=jnp.float32)
    lg = log_gamma[:, None]
    diff = pos[:, None] - pos[None, :]
    decay = jnp.where(diff[None] >= 0, jnp.exp(lg[:, :, None] * jnp.maximum(diff, 0.0)[None]), 0.0)
    xi = jnp.exp(lg * (pos + 1.0))
    zeta = jnp.exp(lg * (RET_CHUNK - 1.0 - pos))
    chunk_decay = jnp.exp(log_gamma * RET_CHUNK)
    scores = jnp.einsum('bhnid,bhnjd->bhnij', qc, kc) * decay[:, None]
    o_intra = jnp.einsum('bhnij,bhnje->bhnie', scores, vc)
    kv = jnp.einsum('bhnjd,bhnje->nbhde', kc * zeta[:, None, :, None], vc)

    def step(r, kv_n):
        return chunk_decay[:, None, None] * r + kv_n, r

    s_fin, r_prev = lax.scan(step, s0.astype(jnp.float32), kv)
    o_cross = jnp.einsum('bhnid,nbhde->bhnie', qc * xi[:, None, :, None], r_prev)
    return (o_intra + o_cross).reshape(b, h, l, dv), s_fin

def bidir_retention(q, k, v, lg_f, lg_b, s0_f, s0_b):
    o_f, s_f = retention_chunkwise(q, k, v, lg_f, s0_f)
    o_b, s_b = retention_chunkwise(jnp.flip(q, 2), jnp.flip(k, 2), jnp.flip(v, 2), lg_b, s0_b)
    return o_f + jnp.flip(o_b, 2), s_f, s_b

def head_norm(o, g):
    mu = jnp.mean(o, axis=-1, keepdims=True)
    var = jnp.mean(jnp.square(o - mu), axis=-1, keepdims=True)
    y = (o - mu) * lax.rsqrt(var + GN_EPS)
    b, h, l, dv = o.shape
    return y.transpose(0, 2, 1, 3).reshape(b, l, h * dv) * g.astype(jnp.float32)

def short_conv3(u, w):
    up = jnp.pad(u, ((0, 0), (1, 1), (0, 0)))
    return up[:, :-2] * w[0] + up[:, 1:-1] * w[1] + up[:, 2:] * w[2]

def mixer(h, s0_f, s0_b, use_rope, w_in, dec_f, dec_b, gn_g, conv_w, w_ret_o, w_conv_o, w_o):
    b, l, _ = h.shape
    proj = h @ w_in
    q, k, v, g_ret, cb, cc, cx, ga, gb = jnp.split(proj, SPLIT_POINTS, axis=-1)
    q = q.reshape(b, l, N_RET_HEADS, RET_DK).transpose(0, 2, 1, 3)
    k = k.reshape(b, l, N_RET_HEADS, RET_DK).transpose(0, 2, 1, 3) * (RET_DK ** -0.5)
    v = v.reshape(b, l, N_RET_HEADS, RET_DV).transpose(0, 2, 1, 3)
    if use_rope:
        q = rope_2d(q)
        k = rope_2d(k)
    lg_f = -jax.nn.softplus(-dec_f.astype(jnp.float32))
    lg_b = -jax.nn.softplus(-dec_b.astype(jnp.float32))
    o, s_f, s_b = bidir_retention(q, k, v, lg_f, lg_b, s0_f, s0_b)
    o = head_norm(o, gn_g).astype(h.dtype)
    y_ret = (jax.nn.silu(g_ret) * o) @ w_ret_o
    u = short_conv3(cc * cx, conv_w)
    y_conv = (cb * u) @ w_conv_o
    merged = jax.nn.sigmoid(ga) * y_ret + jax.nn.sigmoid(gb) * y_conv
    return merged @ w_o, s_f, s_b

def expert_choice_ffn(h, w_router, w_gate, w_up, w_down):
    b, l, d = h.shape
    t = b * l
    cap = EC_CAPACITY_FACTOR * t // N_EXPERTS
    hf = h.reshape(t, d)
    aff = jax.nn.softmax((hf @ w_router).astype(jnp.float32), axis=-1)
    vals, idx = lax.top_k(aff.T, cap)
    xs = hf[idx]
    hid = jax.nn.silu(jnp.einsum('ecd,edf->ecf', xs, w_gate)) * jnp.einsum('ecd,edf->ecf', xs, w_up)
    out = jnp.einsum('ecf,efd->ecd', hid, w_down) * vals[..., None].astype(h.dtype)
    y = jnp.zeros_like(hf).at[idx.reshape(-1)].add(out.reshape(-1, d))
    return y.reshape(b, l, d)

def trunk_layer(x, cond, s0_f, s0_b, use_rope, w_ada, b_ada, n_pre_mix, n_post_mix, n_pre_ffn, n_post_ffn,
                w_in, dec_f, dec_b, gn_g, conv_w, w_ret_o, w_conv_o, w_o, w_router, w_gate, w_up, w_down):
    mod = (jax.nn.silu(cond) @ w_ada + b_ada)[:, None, :]
    sh1, sc1, g1, sh2, sc2, g2 = jnp.split(mod, 6, axis=-1)
    h = rmsnorm(x, n_pre_mix) * (1.0 + sc1) + sh1
    m, s_f, s_b = mixer(h, s0_f, s0_b, use_rope, w_in, dec_f, dec_b, gn_g, conv_w, w_ret_o, w_conv_o, w_o)
    x = x + g1 * rmsnorm(m, n_post_mix)
    h = rmsnorm(x, n_pre_ffn) * (1.0 + sc2) + sh2
    f = expert_choice_ffn(h, w_router, w_gate, w_up, w_down)
    x = x + g2 * rmsnorm(f, n_post_ffn)
    return x, s_f, s_b

def setup_inputs(seed: int = 0) -> dict:
    key = jax.random.key(seed)
    ks = jax.random.split(key, 26)
    f32 = jnp.float32

    def nrm(k, shape, scale):
        return jax.random.normal(k, shape, f32) * scale

    base_logit = jnp.asarray(np.log(2.0 ** (5 + np.arange(N_RET_HEADS)) - 1.0), f32)
    st_shape = (DEC_BATCH, DEPTH, N_RET_HEADS, RET_DK, RET_DV)
    return {
        'x_prompt': nrm(ks[0], (BATCH, SEQ, D_MODEL), 1.0),
        'x_sample': nrm(ks[1], (DEC_BATCH, DEC_SEQ, D_MODEL), 1.0),
        'state_ret_fwd': nrm(ks[2], st_shape, 1.0),
        'state_ret_bwd': nrm(ks[3], st_shape, 1.0),
        'c': nrm(ks[4], (DEC_BATCH, D_MODEL), 1.0),
        'c_ctx': nrm(ks[5], (D_MODEL,), 1.0),
        'w_ada': nrm(ks[6], (DEPTH, D_MODEL, 6 * D_MODEL), 0.5 * D_MODEL ** -0.5),
        'b_ada': nrm(ks[7], (DEPTH, 6 * D_MODEL), 0.02),
        'norm_pre_mix': 1.0 + nrm(ks[8], (DEPTH, D_MODEL), 0.05),
        'norm_post_mix': 1.0 + nrm(ks[9], (DEPTH, D_MODEL), 0.05),
        'norm_pre_ffn': 1.0 + nrm(ks[10], (DEPTH, D_MODEL), 0.05),
        'norm_post_ffn': 1.0 + nrm(ks[11], (DEPTH, D_MODEL), 0.05),
        'w_in': nrm(ks[12], (DEPTH, D_MODEL, D_IN_TOTAL), D_MODEL ** -0.5),
        'ret_decay_fwd': base_logit + nrm(ks[13], (DEPTH, N_RET_HEADS), 0.05),
        'ret_decay_bwd': base_logit + nrm(ks[14], (DEPTH, N_RET_HEADS), 0.05),
        'ret_norm_g': 1.0 + nrm(ks[15], (DEPTH, D_RET_V), 0.05),
        'conv_w': nrm(ks[16], (DEPTH, CONV_W, D_CONV), CONV_W ** -0.5),
        'w_ret_o': nrm(ks[17], (DEPTH, D_RET_V, D_MODEL), D_RET_V ** -0.5),
        'w_conv_o': nrm(ks[18], (DEPTH, D_CONV, D_MODEL), D_CONV ** -0.5),
        'w_o': nrm(ks[19], (DEPTH, D_MODEL, D_MODEL), D_MODEL ** -0.5),
        'w_router': nrm(ks[20], (DEPTH, D_MODEL, N_EXPERTS), D_MODEL ** -0.5),
        'w_gate': nrm(ks[21], (DEPTH, N_EXPERTS, D_MODEL, EXPERT_FF), D_MODEL ** -0.5),
        'w_up': nrm(ks[22], (DEPTH, N_EXPERTS, D_MODEL, EXPERT_FF), D_MODEL ** -0.5),
        'w_down': nrm(ks[23], (DEPTH, N_EXPERTS, EXPERT_FF, D_MODEL), EXPERT_FF ** -0.5),
    }

def reference(x_prompt, x_sample, state_ret_fwd, state_ret_bwd, c, c_ctx, w_ada, b_ada,
              norm_pre_mix, norm_post_mix, norm_pre_ffn, norm_post_ffn, w_in, ret_decay_fwd, ret_decay_bwd,
              ret_norm_g, conv_w, w_ret_o, w_conv_o, w_o, w_router, w_gate, w_up, w_down):
    xp = x_prompt
    xs = x_sample
    new_f = []
    new_b = []
    for l in range(DEPTH):
        lw = (w_ada[l], b_ada[l], norm_pre_mix[l], norm_post_mix[l], norm_pre_ffn[l], norm_post_ffn[l],
              w_in[l], ret_decay_fwd[l], ret_decay_bwd[l], ret_norm_g[l], conv_w[l], w_ret_o[l], w_conv_o[l],
              w_o[l], w_router[l], w_gate[l], w_up[l], w_down[l])
        zeros = jnp.zeros((xp.shape[0], N_RET_HEADS, RET_DK, RET_DV), jnp.float32)
        xp, s_f, s_b = trunk_layer(xp, c_ctx[None, :], zeros, zeros, False, *lw)
        new_f.append(s_f.astype(x_prompt.dtype))
        new_b.append(s_b.astype(x_prompt.dtype))
        xs, _, _ = trunk_layer(xs, c, state_ret_fwd[:, l], state_ret_bwd[:, l], True, *lw)
    new_state_ret_fwd = jnp.stack(new_f, axis=1)
    new_state_ret_bwd = jnp.stack(new_b, axis=1)
    return (xp, xs, new_state_ret_fwd, new_state_ret_bwd)


_drawn_inputs = setup_inputs


def setup_inputs(seed=0):
    import zlib

    import numpy as np

    out = dict(_drawn_inputs(seed))
    spreads = {}
    factors = {'norm_post_ffn': 4.006, 'ret_norm_g': 3.835}
    for name, (base, spread) in spreads.items():
        noise = np.random.default_rng([zlib.crc32(name.encode()), seed]).standard_normal(out[name].shape)
        drawn = base * np.exp(spread * noise) if base else spread * noise
        out[name] = __import__('jax').numpy.asarray(drawn.astype(out[name].dtype))
    for name, factor in factors.items():
        out[name] = (out[name] * factor).astype(out[name].dtype)
    return out
```

```python
from contextlib import ExitStack, contextmanager

import concourse.bass as bass
from concourse import mybir
import numpy as np

ALU = mybir.AluOpType
ACT = mybir.ActivationFunctionType
F32 = mybir.dt.float32
F32R = mybir.dt.float32r
U32 = mybir.dt.uint32
AX_X = mybir.AxisListType.X

P = 128
D = 1024
KD = D // P
CTX, LAT = 128, 1024
TOK = CTX + LAT
NT = TOK // P
HEADS, DK, DV = 8, 64, 128
PAIRS = HEADS // 2
GRID_W = 64
NB = 3
CB = TOK // NB
EXPERTS = 16
CAP_L, CAP_C = 2 * LAT // EXPERTS, 2 * CTX // EXPERTS
CAP = CAP_L + CAP_C
RMS_EPS, GN_EPS = 1e-6, 1e-5

COL_Q, COL_K, COL_V, COL_G, COL_CB, COL_CC, COL_CX, COL_GA, COL_GB = 0, 4, 8, 16, 24, 32, 40, 48, 56

T_RET = 0
T_RETOUT = T_RET + 6 * PAIRS
T_CONV = T_RETOUT + 2 * KD
T_CONVOUT = T_CONV + 3 * KD
T_WO = T_CONVOUT + 2 * KD

EA_RETOUT, ED_RETOUT = 6 * PAIRS, 0
EA_CONV, ED_CONV = EA_RETOUT + KD, ED_RETOUT + KD
EA_CONVOUT, ED_CONVOUT = EA_CONV + 2 * KD, ED_CONV + KD

V_BADA, V_PREMIX, V_POSTMIX, V_PREFFN, V_POSTFFN, V_GN, V_CONV, V_C, V_CCTX = 0, 48, 56, 64, 72, 80, 88, 112, 120
R_G1, R_A2, R_SH2, R_G2 = 0, 1, 2, 3

CHUNKS = [range(0, 1), range(1, 5), range(5, 9)]
ATT = ([("swap_q", x, "D") for x in range(2)] + [("swap_k", x, "D") for x in range(2)]
       + [("k_tok", x, "A") for x in range(3)]
       + [("v_tok0", x, "A") for x in range(3)] + [("dup0", x, "D") for x in range(2)]
       + [("score0", x, "D") for x in range(3)] + [("kv0", x, "D") for x in range(3)]
       + [("o0", x, "D") for x in range(3)]
       + [("v_tok1", x, "A") for x in range(3)] + [("dup1", x, "D") for x in range(2)]
       + [("o_feat0", x, "D") for x in range(3)]
       + [("score1", x, "D") for x in range(3)] + [("kv1", x, "D") for x in range(3)]
       + [("o1", x, "D") for x in range(3)] + [("o_feat1", x, "D") for x in range(3)])
ATT_AT = {(n, x): b for b, (n, x, _) in enumerate(ATT)}
N_ATT = len(ATT)
N_ATT_BY = {e: sum(a[2] == e for a in ATT) for e in "AD"}


def att_reads(name, x):
    b = ATT_AT[name, x]
    return sum(a[2] == ATT[b][2] for a in ATT[:b + 1])


def shape_tables():
    i = np.arange(P)
    f = np.float32
    ident = np.eye(P, dtype=f)
    partner = np.where(i % 32 < 16, i + 16, i - 16)
    swap = (i[:, None] == partner[None, :]).astype(f)
    dup = [(i[:, None] == 64 * h + i[None, :] % 64).astype(f) for h in range(2)]
    xarg = np.where(i[:, None] < DK, i[None, :] + 1, P - i[None, :]).astype(f)
    diff = (i[None, :] - i[:, None]).astype(f)
    fwd, bwd = np.maximum(diff, 0), np.maximum(-diff, 0)
    mfwd, mbwd = (diff >= 0).astype(f), (diff <= 0).astype(f)
    pos = np.stack([P - 1 - i, i, np.full(P, P)], 1).astype(f)
    inv = (f(10000.0) ** (-np.arange(16, dtype=f) / f(16))).astype(f)
    t = np.arange(LAT)
    where = np.where((i % 64 < 32)[:, None], (t // GRID_W)[None, :], (t % GRID_W)[None, :]).astype(f)
    ang = where * inv[i % 16][:, None]
    cos, sin = np.cos(ang).astype(f), np.sin(ang).astype(f)
    sin = np.where((i % 32 < 16)[:, None], -sin, sin)
    small = np.concatenate([ident, swap, dup[0], dup[1], xarg, fwd, bwd, mfwd, mbwd, pos, np.full((P, 4), -0.5, f), np.full((P, 4), GN_EPS, f),
                            np.full((P, 1), RMS_EPS, f)], 1)
    return small.astype(f), np.stack([cos, sin], 1).astype(f)


N_SMALL = 9 * P + 12


class Steps:

    def __init__(self, eng, sem):
        self.eng, self.sem, self.base, self.n = eng, sem, 0, 0

    def did(self, ins):
        ins.then_inc(self.sem, 1)
        self.n += 1

    def settle(self):
        self.eng.wait_ge(self.sem, self.base + self.n)

    @contextmanager
    def loop(self, count, per):
        with self.eng.Fori(0, count) as i:
            before = self.n
            self.base, self.n = before + i * per, 0
            yield i
            assert self.n == per, (self.n, per)
        self.base, self.n = 0, before + count * per


def build(nc, x_prompt, x_sample, state_f, state_b, c, c_ctx, w_ada, b_ada, n_pre_mix, n_post_mix,
          n_pre_ffn, n_post_ffn, w_in, dec_f, dec_b, gn_g, conv_w, w_ret_o, w_conv_o, w_o, w_router,
          w_gate, w_up, w_down, small_tab, rope_tab, y_prompt, y_sample, new_f, new_b):
    with ExitStack() as ctx:
        BASE = 16512

        def at(name, offset, shape, dt=F32):
            return nc.alloc_sbuf_tensor_at(name, shape, dt, offset=BASE + offset)

        def sem(name):
            return ctx.enter_context(nc.semaphore(name))

        def dram(name, shape):
            return nc.dram_tensor(name, shape, F32, kind="Internal").ap()

        FT = TOK * 4
        SL = D * 4
        A_H = 0
        A_W = 2 * KD * FT
        A_ZA = A_W + 6 * SL
        A_ZB = A_ZA + KD * FT
        A_C = A_ZB + KD * FT
        h_hi = at("h_hi", A_H, [P, KD, TOK], F32R)
        h_lo = at("h_lo", A_H + KD * FT, [P, KD, TOK], F32R)
        w_hi = at("w_hi", A_W, [P, 2, KD, P], F32R)
        w_lo = at("w_lo", A_W + 2 * SL, [P, 2, KD, P], F32R)
        w_raw = at("w_raw", A_W + 4 * SL, [P, 2, KD, P])
        z_ret = at("z_ret", A_ZA, [P, HEADS, TOK])
        z_lo = at("z_lo", A_ZA, [P, KD, TOK], F32R)
        z_hi = at("z_hi", A_ZB, [P, KD, TOK], F32R)

        off = A_C
        def const(name, shape, dt=F32):
            nonlocal off
            size = 4
            for n in shape[1:]:
                size *= n
            t = at(name, off, shape, dt)
            off += (size + 31) // 32 * 32
            return t

        small = const("small", [P, N_SMALL])
        ident, swap = small[:, 0:P], small[:, P:2 * P]
        dup = [small[:, (2 + h) * P:(3 + h) * P] for h in range(2)]
        xarg = small[:, 4 * P:5 * P]
        fwd, bwd = small[:, 5 * P:6 * P], small[:, 6 * P:7 * P]
        mfwd, mbwd = small[:, 7 * P:8 * P], small[:, 8 * P:9 * P]
        pos = small[:, 9 * P:9 * P + 3]
        minus_half, gn_eps, rms_eps = (small[:, 9 * P + a:9 * P + b] for a, b in ((3, 7), (7, 11), (11, 12)))
        vecT = const("vecT", [P, P])
        modT = const("modT", [P, 48, 2])
        scale1 = const("scale1", [P, KD, 2])
        cond = const("cond", [P, KD, 2])
        lg = const("lg", [P, 3, HEADS])
        lgt = const("lgt", [P, 5, 3, HEADS])
        zeta = const("zeta", [P, 2, HEADS])
        zeta2 = const("zeta2", [P, 2, 2])
        gchunk = const("gchunk", [P, HEADS])
        decay = const("decay", [P, HEADS, P])
        xi = const("xi", [P, HEADS, P])
        stats = const("stats", [P, 64])
        gn6 = const("gn6", [P, NT, 6])
        gnmv = const("gnmv", [P, NT, 2])
        gnr = const("gnr", [P, NT])
        state_out = const("state_out", [P, P])
        A_S = off
        rope = at("rope", A_S, [P, 2, LAT])

        names = ["qT", "kT", "kz0", "kz1", "vT", "v_tok", "sm", "on"]
        ret = {n: at(n, A_ZB + j * FT, [P, NT, P]) for j, n in enumerate(names)}
        qT, kT, v_tok, sm, on = ret["qT"], ret["kT"], ret["v_tok"], ret["sm"], ret["on"]
        vT = ret["vT"]
        kz = [ret["kz0"], ret["kz1"]]
        A_S2 = A_S + 2 * SL
        tmp = at("tmp", A_S2, [P, LAT])
        qx = at("qx", A_S2 + SL, [P, LAT // P, P])
        rs = at("rs", A_S2 + 2 * SL, [P, LAT // P, P])
        s0 = at("s0", A_S2 + 3 * SL, [P, HEADS, P])
        assert BASE + A_S2 + 4 * SL <= nc.sbuf_usable_end, (BASE + A_S2 + 4 * SL, nc.sbuf_usable_end)

        ada = [at(f"ada{j}", A_ZA + j * KD * SL, [P, KD, D]) for j in range(2)]
        A_X = A_W
        x_in = [at(f"x_in{j}", A_X + j * SL, [P, KD, P]) for j in range(2)]
        hf = at("hf", A_X + 2 * SL, [P, KD, P])
        sq = at("sq", A_X + 3 * SL, [P, D])
        e2 = at("e2", A_ZA + 2 * KD * SL, [P, HEADS, P])
        vec_in = at("vec_in", A_ZA + 2 * KD * SL + SL, [P, P])
        rowsT = at("rowsT", A_ZA + 2 * KD * SL + SL + 512, [P, 64])
        rows = at("rows", A_ZA + 2 * KD * SL + SL + 768, [64, P])

        gate = at("gate", A_S, [P, TOK])
        merged = at("merged", A_S + FT, [P, TOK])
        ret_part = at("ret_part", A_S + 2 * FT, [P, TOK])
        cbT = at("cbT", A_S, [P, TOK])
        ccT = at("ccT", A_S + FT, [P, TOK])
        prod = at("prod", A_S + 2 * FT, [P, TOK + 8])
        u = at("u", A_S + 3 * FT + 32, [P, TOK + 8])

        wo_hi = at("wo_hi", A_H, [P, KD, D], F32R)
        wo_lo = at("wo_lo", A_H + KD * SL, [P, KD, D], F32R)
        Z = A_ZA
        m_raw = [at(f"m_raw{j}", Z + j * SL, [P, KD, P]) for j in range(2)]
        m_hi = [at(f"m_hi{j}", Z + (2 + j) * SL, [P, KD, P], F32R) for j in range(2)]
        m_lo = [at(f"m_lo{j}", Z + (4 + j) * SL, [P, KD, P], F32R) for j in range(2)]
        x_res = [at(f"x_res{j}", Z + (6 + j) * SL, [P, D]) for j in range(2)]
        tabs = at("tabs", Z + 8 * SL, [P, 6, D])
        x1 = [at(f"x1_{j}", Z + (14 + j) * SL, [P, D]) for j in range(2)]
        h2 = [at(f"h2_{j}", Z + (16 + j) * SL, [P, D]) for j in range(2)]
        h2T = at("h2T", A_S, [P, KD, P])
        sq2 = at("sq2", A_S + SL, [P, D])
        w_rt = at("w_rt", A_S + 2 * SL, [P, KD, EXPERTS])
        aff = at("aff", A_S + 2 * SL + 512, [P, NT, EXPERTS])
        affT = at("affT", A_S + 3 * SL, [EXPERTS, TOK])
        sel_v = at("sel_v", A_S + 3 * SL + FT, [EXPERTS, CAP])
        sel_i = at("sel_i", A_S + 3 * SL + FT + 576, [EXPERTS, CAP], U32)
        sel_f = at("sel_f", A_S + 3 * SL + FT + 1152, [EXPERTS, CAP])
        val_l = at("val_l", A_S + 2 * SL + 1152, [P, EXPERTS])
        val_c = at("val_c", A_S + 2 * SL + 1152 + 64, [CAP_C, EXPERTS])
        idx_l = at("idx_l", A_S + 2 * SL + 1152 + 128, [P, EXPERTS], U32)
        idx_c = at("idx_c", A_S + 2 * SL + 1152 + 192, [CAP_C, EXPERTS], U32)

        wq = [at(f"wq{j}", j * 2 * SL, [P, KD, 2 * P]) for j in range(12)]
        xg_l = at("xg_l", Z, [P, D])
        xg_c = at("xg_c", Z + SL, [CAP_C, D])
        xT = at("xT", Z + 2 * SL, [P, KD, CAP])
        sg = at("sg", Z + 2 * SL + 4608, [P, 2, CAP])
        hid = at("hid", Z + 3 * SL + 4608, [P, KD, CAP])
        outT = at("outT", Z + 3 * SL + 2 * 4608, [P, KD, CAP])
        ot_l = at("ot_l", Z + 3 * SL + 3 * 4608, [P, D])
        ot_c = at("ot_c", Z + 4 * SL + 3 * 4608, [CAP_C, D])
        zero = at("zero", A_S, [P, D])
        g2 = at("g2", Z + 8 * SL, [P, 2, D])
        f_in = [at(f"f_in{j}", Z + (10 + j) * SL, [P, D]) for j in range(2)]
        x1_in = [at(f"x1_in{j}", Z + (12 + j) * SL, [P, D]) for j in range(2)]
        y_out = [at(f"y_out{j}", Z + (14 + j) * SL, [P, D]) for j in range(2)]
        sq3 = at("sq3", Z + 16 * SL, [P, D])

        ps = ctx.enter_context(nc.psum_tensor("ps", [P, 8, 512], F32))

        rows_d = dram("rows_d", [8, D])
        merged_d = dram("merged_d", [KD, P, TOK])
        x1_d = dram("x1_d", [NT, P, D])
        h2_d = dram("h2_d", [TOK, D])
        ffn_d = dram("ffn_d", [TOK, D])

        xp = x_prompt[0]
        xs = x_sample[0].rearrange("(t p) d -> t p d", p=P)
        yp = y_prompt[0]
        ys = y_sample[0].rearrange("(t p) d -> t p d", p=P)

        def cols(w, j):
            return w[:, bass.ds(j * P, P)].rearrange("(k p) n -> p k n", p=P)

        small_in, vec_in_s, dec_in, rope_in, s0_in = (sem(n) for n in ("small_in", "vec_in_s", "dec_in", "rope_in", "s0_in"))
        ada_in = [sem(f"ada_in{j}") for j in range(2)]
        x_in_s = [sem(f"x_in_s{j}") for j in range(2)]
        w_in_s = [sem(f"w_landed{j}") for j in range(2)]
        act_step, dve_step, pool_step = sem("act_step"), sem("dve_step"), sem("pool_step")
        vec_turned, vec_ready, cond_ready = sem("vec_turned"), sem("vec_ready"), sem("cond_ready")
        ada_done, ada_read = sem("ada_done"), sem("ada_read")
        rows_made, rows_turned, rows_ready, rows_stored = sem("rows_made"), sem("rows_turned"), sem("rows_ready"), sem("rows_stored")
        x_norm, x_turned, x_mod, h_hi_done, h_lo_done = (sem(n) for n in ("x_norm", "x_turned", "x_mod", "h_hi_done", "h_lo_done"))
        ss_done, rstd_done = sem("ss_done"), sem("rstd_done")
        lg_part, lg_exp, lg_ready, exp_ready = sem("lg_part"), sem("lg_exp"), sem("lg_ready"), sem("exp_ready")
        w_hi_done, w_lo_done, projected = sem("w_hi_done"), sem("w_lo_done"), sem("projected")
        act_evicted, dve_evicted = sem("act_evicted"), sem("dve_evicted")
        att_made, att_act, att_dve = sem("att_made"), sem("att_act"), sem("att_dve")
        roped, state_ready, state_stored = sem("roped"), sem("state_ready"), sem("state_stored")
        z_hi_done, z_lo_done = sem("z_hi_done"), sem("z_lo_done")
        merged_ready, merged_stored, ret_part_in = sem("merged_ready"), sem("merged_stored"), sem("ret_part_in")
        conv_z, conv_z_raw = sem("conv_z"), sem("conv_z_raw")
        wo_hi_done, wo_lo_done = sem("wo_hi_done"), sem("wo_lo_done")
        tabs_in, router_in = sem("tabs_in"), sem("router_in")
        m_in = [sem(f"m_in{j}") for j in range(2)]
        xr_in = [sem(f"xr_in{j}") for j in range(2)]
        m_hi_done, m_lo_done, m_made, m_sq = sem("m_hi_done"), sem("m_lo_done"), sem("m_made"), sem("m_sq")
        x1_ready, x1_sq, h2_ready = sem("x1_ready"), sem("x1_sq"), sem("h2_ready")
        x1_stored, h2_stored = ([sem(f"{n}{j}") for j in range(2)] for n in ("x1_stored", "h2_stored"))
        h2_turned, h2T_ready, logit_made, logit_max, logit_exp, aff_done = (
            sem(n) for n in ("h2_turned", "h2T_ready", "logit_made", "logit_max", "logit_exp", "aff_done"))
        aff_turned, affT_ready, sel_ready, sel_turned, sel_read = (
            sem(n) for n in ("aff_turned", "affT_ready", "sel_ready", "sel_turned", "sel_read"))
        zero_ready, ffn_zeroed = sem("zero_ready"), sem("ffn_zeroed")
        wq_in = [sem(f"wq_in{j}") for j in range(12)]
        unit_made, unit_act, unit_dve = sem("unit_made"), sem("unit_act"), sem("unit_dve")
        got_l, got_c = sem("got_l"), sem("got_c")
        xg_turned, xT_ready, out_turned, out_ready = sem("xg_turned"), sem("xT_ready"), sem("out_turned"), sem("out_ready")
        added_l, added_c = sem("added_l"), sem("added_c")
        g2_in = sem("g2_in")
        f_in_s = [sem(f"f_in_s{j}") for j in range(2)]
        x1_in_s = [sem(f"x1_in_s{j}") for j in range(2)]
        f_sq, f_rstd, y_ready = sem("f_sq"), sem("f_rstd"), sem("y_ready")
        m_rstd, x1_rstd, gn_var, gn_rstd = sem("m_rstd"), sem("x1_rstd"), sem("gn_var"), sem("gn_rstd")
        y_stored = [sem(f"y_stored{j}") for j in range(2)]

        tally = {}

        def plain(eng):
            name = str(eng.engine).split(".")[-1]
            if name not in tally:
                tally[name] = eng.alloc_register(f"tally_{name}")
                eng.reg_mov(tally[name], 0)
            eng.reg_add(tally[name], tally[name], 1)

        block = ctx.enter_context(nc.Block())

        @block.sync
        def _(sp):
            sp.dma_start(small[:], small_tab).then_inc(small_in, 16)
            for row, v in ((V_BADA, b_ada[0]), (V_PREMIX, n_pre_mix[0]), (V_POSTMIX, n_post_mix[0]),
                           (V_PREFFN, n_pre_ffn[0]), (V_POSTFFN, n_post_ffn[0]), (V_GN, gn_g[0]),
                           (V_CONV, conv_w[0].rearrange("t d -> (t d)")), (V_C, c[0]), (V_CCTX, c_ctx)):
                n = v.shape[0] // P
                sp.dma_start(vec_in[row:row + n, :], v.rearrange("(r p) -> r p", p=P)).then_inc(vec_in_s, 16)

            def load_ada(j):
                if j >= 2:
                    sp.wait_ge(ada_done, j - 1)
                sp.dma_start(ada[j % 2][:], w_ada[0][:, j * D:(j + 1) * D].rearrange("(k p) n -> p k n", p=P))\
                  .then_inc(ada_in[j % 2], 16)

            load_ada(0)
            load_ada(1)

            for j in range(2, 6):
                load_ada(j)

            def load_w(i, t0, per, c_, src):
                sp.wait_ge(w_lo_done, t0 + per * i + c_ - 1)
                sp.dma_start(w_raw[:, c_ % 2], src).then_inc(w_in_s[c_ % 2], 16)

            w = w_in[0]
            sp.dma_start(rope[:], rope_tab).then_inc(rope_in, 16)
            with sp.Fori(0, PAIRS) as i:
                for c_, col in enumerate((COL_Q + i, COL_K + i, COL_V + 2 * i, COL_G + 2 * i,
                                          COL_V + 2 * i + 1, COL_G + 2 * i + 1)):
                    if c_ == 0:
                        sp.wait_ge(w_lo_done, 6 * i)
                    elif c_ >= 2:
                        sp.wait_ge(w_lo_done, 6 * i + c_ - 1)
                    sp.dma_start(w_raw[:, c_ % 2], cols(w, col)).then_inc(w_in_s[c_ % 2], 16)
            with sp.Fori(0, KD) as i:
                load_w(i, T_RETOUT, 2, 0, cols(w, COL_GA + i))
                load_w(i, T_RETOUT, 2, 1, cols(w_ret_o[0], i))
            with sp.Fori(0, KD // 2) as i:
                for c_ in range(6):
                    load_w(i, T_CONV, 6, c_, cols(w, (COL_CB, COL_CC, COL_CX)[c_ % 3] + 2 * i + c_ // 3))
            with sp.Fori(0, KD) as i:
                load_w(i, T_CONVOUT, 2, 0, cols(w, COL_GB + i))
                load_w(i, T_CONVOUT, 2, 1, cols(w_conv_o[0], i))
            for k in range(KD):
                if k < 2:
                    sp.wait_ge(w_lo_done, T_WO + k - 1)
                else:
                    sp.wait_ge(wo_lo_done, k - 1)
                sp.dma_start(w_raw[:, k % 2], w_o[0][k * P:(k + 1) * P, :].rearrange("p (k n) -> p k n", n=P))\
                  .then_inc(w_in_s[k % 2], 16)

            sp.wait_ge(projected, T_WO)
            sp.wait_ge(rows_stored, 16)
            for j in range(6):
                sp.dma_start(tabs[:, j, :], rows_d[j:j + 1, :].broadcast_to([P, D])).then_inc(tabs_in, 16)
            sp.wait_ge(merged_stored, 16 * 2 * KD)

            def load_m(t, b, src):
                sp.dma_start(m_raw[b][:], merged_d[:, :, bass.ds(t * P, P)].rearrange("k p n -> p k n")).then_inc(m_in[b], 16)
                sp.dma_start(x_res[b][:], src).then_inc(xr_in[b], 16)

            load_m(0, 0, xp)
            load_m(1, 1, xs[0])
            sp.dma_start(w_rt[:], w_router[0].rearrange("(k p) e -> p k e", p=P)).then_inc(router_in, 16)

            def load_unit(e, j, first):
                w3 = (w_gate, w_up)[j % 2] if j < 8 else w_down
                q = j // 2 if j < 8 else j - 8
                if not first:
                    sp.wait_ge(unit_made, 12 * e - 12 + j + 1)
                sp.dma_start(wq[j][:], w3[0][bass.ds(e, 1), :, q * 2 * P:(q + 1) * 2 * P]
                             .rearrange("a (k p) n -> p (a k) n", p=P)).then_inc(wq_in[j], 16)

            sp.wait_ge(wo_lo_done, KD)
            for j in range(8, 12):
                load_unit(0, j, True)
            def load_m_when_free(t, b, src):
                sp.wait_ge(m_lo_done, t - 1)
                sp.wait_ge(x1_ready, t - 1)
                load_m(t, b, src)

            with sp.Fori(0, 3) as i:
                for b in range(2):
                    load_m_when_free(2 * i + b + 2, b, xs[bass.ds(2 * i + b + 1, 1)].rearrange("a p d -> (a p) d"))
            load_m_when_free(8, 0, xs[7])

            sp.wait_ge(m_made, NT)
            for j in range(8):
                load_unit(0, j, True)
            with sp.Fori(1, EXPERTS) as e:
                for j in range(12):
                    load_unit(e, j, False)

            sp.wait_ge(added_l, 16 * EXPERTS)
            sp.wait_ge(added_c, 16 * EXPERTS)
            for j in range(2):
                sp.dma_start(g2[:, j, :], rows_d[6 + j:7 + j, :].broadcast_to([P, D])).then_inc(g2_in, 16)

            def load_f(t, b):
                sp.dma_start(f_in[b][:], ffn_d[bass.ds(t * P, P), :]).then_inc(f_in_s[b], 16)
                sp.dma_start(x1_in[b][:], x1_d[bass.ds(t, 1)].rearrange("a p d -> (a p) d")).then_inc(x1_in_s[b], 16)

            load_f(0, 0)
            load_f(1, 1)
            with sp.Fori(0, 3) as i:
                for b in range(2):
                    sp.wait_ge(y_ready, 2 * i + b + 1)
                    load_f(2 * i + b + 2, b)
            sp.wait_ge(y_ready, 7)
            load_f(8, 0)

        @block.gpsimd
        def _(pool):
            pool.dma_start(lgt[:, 0, 0, :], dec_f[0:1, :].broadcast_to([P, HEADS])).then_inc(dec_in, 16)
            pool.dma_start(lgt[:, 0, 1, :], dec_b[0:1, :].broadcast_to([P, HEADS])).then_inc(dec_in, 16)
            pool.dma_start(lgt[0:DK, 0, 2, :], dec_f[0:1, :].broadcast_to([DK, HEADS])).then_inc(dec_in, 16)
            pool.dma_start(lgt[DK:P, 0, 2, :], dec_b[0:1, :].broadcast_to([DK, HEADS])).then_inc(dec_in, 16)

            pool_steps = Steps(pool, pool_step)

            def rstd(dst, src, eps):
                pool_steps.did(pool.tensor_tensor(dst, src, eps, ALU.add))
                pool_steps.settle()
                return pool.tensor_tensor(dst, dst, minus_half[:, 0:dst.shape[-1]], ALU.pow)

            pool.wait_ge(small_in, 16)

            def rstd_x(n, b):
                pool.wait_ge(ss_done, n + 1)
                rstd(stats[:, 2 + b:3 + b], stats[:, b:b + 1], rms_eps).then_inc(rstd_done, 1)

            def load_x(t, src):
                pool.dma_start(x_in[t % 2][:].rearrange("p k n -> p (k n)"), src).then_inc(x_in_s[t % 2], 16)

            load_x(0, xp)
            load_x(1, xs[0])
            pool.dma_start(s0[0:DK, :, :], state_f[0, 0].rearrange("h d e -> d h e")).then_inc(s0_in, 16)
            pool.dma_start(s0[DK:P, :, :], state_b[0, 0].rearrange("h d e -> d h e")).then_inc(s0_in, 16)
            rstd_x(0, 0)
            rstd_x(1, 1)
            with pool_steps.loop(3, 2) as i:
                for b in range(2):
                    pool.wait_ge(x_turned, 2 * i + b + 1)
                    plain(pool)
                    pool.dma_start(x_in[b][:].rearrange("p k n -> p (k n)"), xs[bass.ds(2 * i + b + 1, 1)].rearrange("a p d -> (a p) d"))\
                        .then_inc(x_in_s[b], 16)
                    rstd_x(2 * i + b + 2, b)
            pool.wait_ge(x_turned, 7)
            load_x(8, xs[7])
            rstd_x(8, 0)
            pool.wait_ge(rows_ready, 1)
            pool.dma_start(rows_d.rearrange("a (k p) -> (a k) p", p=P), rows[:]).then_inc(rows_stored, 16)

            with pool_steps.loop(HEADS, 3) as h:
                pool.wait_ge(state_ready, h + 1)
                plain(pool)
                pool.dma_start(new_f[0, 0, bass.ds(h, 1)].rearrange("a d e -> (a d) e"), state_out[0:DK, :]).then_inc(state_stored, 16)
                plain(pool)
                pool.dma_start(new_b[0, 0, bass.ds(h, 1)].rearrange("a d e -> (a d) e"), state_out[DK:P, :]).then_inc(state_stored, 16)
                for x in range(3):
                    pool.wait_ge(gn_var, 3 * h + x + 1)
                    ts = slice(CHUNKS[x][0], CHUNKS[x][-1] + 1)
                    rstd(gnr[:, ts], gnmv[:, ts, 1], gn_eps[:, 0:len(CHUNKS[x])]).then_inc(gn_rstd, 1)
            with pool.Fori(0, KD) as n:
                pool.wait_ge(dve_evicted, ED_RETOUT + n + 1)
                pool.wait_ge(merged_stored, 16 * n)
                plain(pool)
                pool.dma_start(merged_d[bass.ds(n, 1)].rearrange("a p t -> (a p) t"), merged[:]).then_inc(merged_stored, 16)
            pool.wait_ge(projected, T_CONVOUT)
            for n in range(KD):
                pool.wait_ge(merged_ready, n)
                pool.wait_ge(conv_z, KD)
                pool.wait_ge(merged_stored, 16 * (KD + n))
                pool.dma_start(ret_part[:], merged_d[n]).then_inc(ret_part_in, 16)
                pool.wait_ge(merged_ready, n + 1)
                pool.dma_start(merged_d[n], merged[:]).then_inc(merged_stored, 16)

            def store(t, b):
                pool.wait_ge(m_sq, t + 1)
                rstd(stats[:, 8 + b:9 + b], stats[:, 4 + b:5 + b], rms_eps).then_inc(m_rstd, 1)
                pool.wait_ge(x1_ready, t + 1)
                plain(pool)
                pool.dma_start(x1_d[bass.ds(t, 1)].rearrange("a p d -> (a p) d"), x1[b][:]).then_inc(x1_stored[b], 16)
                pool.wait_ge(x1_sq, t + 1)
                rstd(stats[:, 12 + b:13 + b], stats[:, 6 + b:7 + b], rms_eps).then_inc(x1_rstd, 1)
                pool.wait_ge(h2_ready, t + 1)
                plain(pool)
                pool.dma_start(h2_d[bass.ds(t * P, P), :], h2[b][:]).then_inc(h2_stored[b], 16)

            with pool_steps.loop(4, 4) as i:
                store(2 * i, 0)
                store(2 * i + 1, 1)
            store(8, 0)
            pool.wait_ge(logit_made, NT)
            pool.memset(zero[:], 0.0).then_inc(zero_ready, 1)
            pool.wait_ge(zero_ready, 1)
            with pool.Fori(0, NT) as t:
                plain(pool)
                pool.dma_start(ffn_d[bass.ds(t * P, P), :], zero[:]).then_inc(ffn_zeroed, 16)
            pool.wait_ge(ffn_zeroed, 16 * NT)
            for b in range(2):
                pool.wait_ge(x1_stored[b], 16 * (5 - b))
                pool.wait_ge(h2_stored[b], 16 * (5 - b))

            def gather(e):
                if e:
                    pool.wait_ge(xg_turned, e)
                pool.indirect_dma_start(xg_l[:], None, h2_d, bass.IndirectOffsetOnAxis(ap=idx_l[:, e:e + 1], axis=0))\
                    .then_inc(got_l, 16)
                pool.indirect_dma_start(xg_c[:], None, h2_d, bass.IndirectOffsetOnAxis(ap=idx_c[:, e:e + 1], axis=0))\
                    .then_inc(got_c, 16)

            pool.wait_ge(sel_read, 4)
            gather(0)
            for e in range(EXPERTS):
                if e + 1 < EXPERTS:
                    gather(e + 1)
                pool.wait_ge(out_ready, 2 * e + 2)
                if e:
                    pool.wait_ge(added_l, 16 * e)
                    pool.wait_ge(added_c, 16 * e)
                pool.indirect_dma_start(ffn_d, bass.IndirectOffsetOnAxis(ap=idx_l[:, e:e + 1], axis=0), ot_l[:], None,
                                        compute_op=ALU.add).then_inc(added_l, 16)
                pool.indirect_dma_start(ffn_d, bass.IndirectOffsetOnAxis(ap=idx_c[:, e:e + 1], axis=0), ot_c[:], None,
                                        compute_op=ALU.add).then_inc(added_c, 16)

            def store_y(t, b, dst):
                pool.wait_ge(f_sq, t + 1)
                rstd(stats[:, 18 + b:19 + b], stats[:, 16 + b:17 + b], rms_eps).then_inc(f_rstd, 1)
                pool.wait_ge(y_ready, t + 1)
                pool.dma_start(dst, y_out[b][:]).then_inc(y_stored[b], 16)

            store_y(0, 0, yp)
            with pool_steps.loop(4, 2) as i:
                store_y(2 * i + 1, 1, ys[bass.ds(2 * i, 1)].rearrange("a p d -> (a p) d"))
                store_y(2 * i + 2, 0, ys[bass.ds(2 * i + 1, 1)].rearrange("a p d -> (a p) d"))
            pool.wait_ge(y_stored[0], 16 * 5)
            pool.wait_ge(y_stored[1], 16 * 4)
            pool.wait_ge(state_stored, 32 * HEADS)

        @block.tensor
        def _(pe):
            def bank(b, n):
                return ps[:, b, 0:n]

            pe.wait_ge(small_in, 16)
            pe.wait_ge(vec_in_s, 16 * 9)
            pe.transpose(bank(6, P), vec_in[:], ident).then_inc(vec_turned, 1)

            def modulation(j):
                if j == 0:
                    pe.wait_ge(cond_ready, 1)
                pe.wait_ge(ada_in[j % 2], 16 * (j // 2 + 1))
                for m in range(KD):
                    for k in range(KD):
                        mm = pe.matmul(ps[:, j, 2 * m:2 * m + 2], ada[j % 2][:, k, m * P:(m + 1) * P], cond[:, k, :],
                                       start=(k == 0), stop=(k == KD - 1))
                mm.then_inc(ada_done, 1)

            modulation(0)
            modulation(1)

            def turn_x(n, b):
                pe.wait_ge(x_norm, n + 1)
                pe.wait_ge(x_mod, n)
                for k in range(KD):
                    tr = pe.transpose(ps[:, 6 + k // 4, (k % 4) * P:(k % 4 + 1) * P], x_in[b][:, k, :], ident)
                tr.then_inc(x_turned, 1)

            with pe.Fori(0, 4) as i:
                turn_x(2 * i, 0)
                turn_x(2 * i + 1, 1)
            turn_x(8, 0)
            for j in range(2, 6):
                modulation(j)
            pe.wait_ge(rows_made, 1)
            pe.wait_ge(x_mod, NT)
            pe.transpose(ps[0:64, 6, 0:P], rowsT[:], ident).then_inc(rows_turned, 1)
            pe.wait_ge(rows_ready, 1)

            def project(t, slot, hi, lo):
                pe.wait_ge(w_lo_done, t + 1)
                for b in range(NB):
                    for k in range(KD):
                        out = ps[:, 3 * slot + b, 0:CB]
                        xh, xl = hi[:, k, b * CB:(b + 1) * CB], lo[:, k, b * CB:(b + 1) * CB]
                        pe.matmul(out, w_hi[:, slot, k, :], xh, start=(k == 0), stop=False)
                        pe.matmul(out, w_hi[:, slot, k, :], xl, start=False, stop=False)
                        mm = pe.matmul(out, w_lo[:, slot, k, :], xh, start=False, stop=(k == KD - 1))
                mm.then_inc(projected, 1)

            pe.wait_ge(h_lo_done, NT)
            with pe.Fori(0, PAIRS) as i:
                def att(name, products):
                    for x in range(3):
                        if (name, x) not in ATT_AT:
                            continue
                        b = ATT_AT[name, x]
                        if b == 0:
                            pe.wait_ge(att_dve, N_ATT_BY["D"] * i)
                            pe.wait_ge(att_act, N_ATT_BY["A"] * i)
                        elif b >= 2:
                            n2, x2, who = ATT[b - 2]
                            pe.wait_ge(att_act if who == "A" else att_dve, N_ATT_BY[who] * i + att_reads(n2, x2))
                        mm = products(x, 6 + b % 2)
                        mm.then_inc(att_made, 1)

                def q_or_k(t, slot):
                    pe.wait_ge(act_evicted, 6 * i + t - 1) if t >= 2 else pe.wait_ge(act_evicted, 6 * i)
                    project(6 * i + t, slot, h_hi, h_lo)

                def halves(lhsT, src):
                    def products(x, b):
                        return pe.matmul(bank(b, 512), lhsT, src[:, 1 + 4 * x:5 + 4 * x, :], start=True, stop=True)
                    return products

                def turns(src):
                    def products(x, b):
                        for s, t in enumerate(CHUNKS[x]):
                            mm = pe.transpose(ps[:, b, s * P:(s + 1) * P], src[:, t, :], ident)
                        return mm
                    return products

                def scores(h):
                    def products(x, b):
                        r = slice(DK * h, DK * h + DK)
                        for s, t in enumerate(CHUNKS[x]):
                            mm = pe.matmul(ps[:, b, s * P:(s + 1) * P], kT[r, t, :], qT[r, t, :], start=True, stop=True)
                        return mm
                    return products

                def key_values(h):
                    def products(x, b):
                        for s, t in enumerate(CHUNKS[x]):
                            mm = pe.matmul(ps[:, b, s * P:(s + 1) * P], kz[h][:, t, :], v_tok[:, t, :], start=True, stop=True)
                        return mm
                    return products

                def outputs(x, b):
                    for s, t in enumerate(CHUNKS[x]):
                        o = ps[:, b, s * P:(s + 1) * P]
                        mm = pe.matmul(o, sm[:, t, :], v_tok[:, t, :], start=True, stop=(t == 0))
                        if t:
                            mm = pe.matmul(o, qx[:, t - 1, :], rs[:, t - 1, :], start=False, stop=True)
                    return mm

                q_or_k(0, 0)
                q_or_k(1, 1)
                q_or_k(2, 0)
                pe.wait_ge(act_evicted, 6 * i + 2)
                att("swap_q", halves(swap, qT))
                att("swap_k", halves(swap, kT))
                q_or_k(3, 1)
                pe.wait_ge(roped, 2 * i + 2)
                att("k_tok", turns(kT))
                pe.wait_ge(act_evicted, 6 * i + 3)
                att("v_tok0", turns(vT))
                att("dup0", halves(dup[0], qT))
                q_or_k(4, 0)
                att("score0", scores(0))
                pe.wait_ge(att_act, N_ATT_BY["A"] * i + att_reads("v_tok0", 2))
                att("kv0", key_values(0))
                q_or_k(5, 1)
                pe.wait_ge(att_dve, N_ATT_BY["D"] * i + att_reads("kv0", 2))
                att("o0", outputs)
                pe.wait_ge(act_evicted, 6 * i + 5)
                att("v_tok1", turns(vT))
                att("dup1", halves(dup[1], qT))
                pe.wait_ge(att_dve, N_ATT_BY["D"] * i + att_reads("o0", 2))
                att("o_feat0", turns(on))
                att("score1", scores(1))
                pe.wait_ge(att_act, N_ATT_BY["A"] * i + att_reads("v_tok1", 2))
                att("kv1", key_values(1))
                pe.wait_ge(att_dve, N_ATT_BY["D"] * i + att_reads("kv1", 2))
                att("o1", outputs)
                pe.wait_ge(att_dve, N_ATT_BY["D"] * i + att_reads("o1", 2))
                att("o_feat1", turns(on))

            with pe.Fori(0, KD) as n:
                pe.wait_ge(act_evicted, EA_RETOUT + n)
                project(T_RETOUT + 2 * n, 0, h_hi, h_lo)
                pe.wait_ge(z_lo_done, KD)
                pe.wait_ge(dve_evicted, ED_RETOUT + n)
                project(T_RETOUT + 2 * n + 1, 1, z_hi, z_lo)
            with pe.Fori(0, KD // 2) as i:
                a, d, t = EA_CONV + 4 * i, ED_CONV + 2 * i, T_CONV + 6 * i
                for c_, (who, n) in enumerate(((act_evicted, a), (dve_evicted, d), (act_evicted, a + 1),
                                               (act_evicted, a + 2), (dve_evicted, d + 1), (act_evicted, a + 3))):
                    pe.wait_ge(who, n)
                    project(t + c_, c_ % 2, h_hi, h_lo)
            with pe.Fori(0, KD) as n:
                pe.wait_ge(act_evicted, EA_CONVOUT + n)
                project(T_CONVOUT + 2 * n, 0, h_hi, h_lo)
                pe.wait_ge(conv_z, KD)
                pe.wait_ge(dve_evicted, ED_CONVOUT + n)
                project(T_CONVOUT + 2 * n + 1, 1, z_hi, z_lo)

            def mix(n, b, half):
                if half == 0:
                    pe.wait_ge(m_lo_done, n + 1)
                for k in range(KD):
                    out = ps[:, 2 * b + half, :]
                    wh, wl = wo_hi[:, k, half * 512:half * 512 + 512], wo_lo[:, k, half * 512:half * 512 + 512]
                    pe.matmul(out, m_hi[b][:, k, :], wh, start=(k == 0), stop=False)
                    pe.matmul(out, m_hi[b][:, k, :], wl, start=False, stop=False)
                    mm = pe.matmul(out, m_lo[b][:, k, :], wh, start=False, stop=(k == KD - 1))
                if half:
                    mm.then_inc(m_made, 1)

            def turn_h2(n, b):
                pe.wait_ge(h2_ready, n + 1)
                pe.wait_ge(h2T_ready, n)
                for k in range(KD):
                    tr = pe.transpose(ps[:, 4 + k // 4, (k % 4) * P:(k % 4 + 1) * P], h2[b][:, k * P:(k + 1) * P], ident)
                tr.then_inc(h2_turned, 1)

            def route(n):
                pe.wait_ge(h2T_ready, n + 1)
                pe.wait_ge(logit_exp, n)
                for k in range(KD):
                    mm = pe.matmul(ps[:, 6, 0:EXPERTS], h2T[:, k, :], w_rt[:, k, :], start=(k == 0), stop=(k == KD - 1))
                mm.then_inc(logit_made, 1)

            pe.wait_ge(wo_lo_done, KD)
            pe.wait_ge(router_in, 16)
            pe.wait_ge(act_evicted, EA_CONVOUT + KD)
            pe.wait_ge(dve_evicted, ED_CONVOUT + KD)
            mix(0, 0, 0)
            mix(0, 0, 1)
            with pe.Fori(0, 4) as i:
                for b in range(2):
                    n = 2 * i + b + 1
                    pe.wait_ge(x1_ready, n - 1)
                    mix(n, 1 - b, 0)
                    turn_h2(n - 1, b)
                    mix(n, 1 - b, 1)
                    route(n - 1)
            turn_h2(8, 0)
            route(8)
            pe.wait_ge(aff_done, NT)
            for t in range(NT):
                tr = pe.transpose(ps[0:EXPERTS, t // 4, (t % 4) * P:(t % 4 + 1) * P], aff[:, t, :], ident)
            tr.then_inc(aff_turned, 1)
            pe.wait_ge(sel_ready, 2)
            id16 = ident[0:EXPERTS, 0:EXPERTS]
            pe.transpose(ps[:, 4, 0:EXPERTS], sel_v[:, 0:CAP_L], id16)
            pe.transpose(ps[0:CAP_C, 4, 16:16 + EXPERTS], sel_v[:, CAP_L:CAP], id16)
            pe.transpose(ps[:, 4, 32:32 + EXPERTS], sel_f[:, 0:CAP_L], id16)
            pe.transpose(ps[0:CAP_C, 4, 48:48 + EXPERTS], sel_f[:, CAP_L:CAP], id16).then_inc(sel_turned, 1)

            def turn_rows(e):
                pe.wait_ge(got_l, 16 * (e + 1))
                pe.wait_ge(got_c, 16 * (e + 1))
                for k in range(KD):
                    pe.transpose(ps[:, 4 + k // 4, (k % 4) * P:(k % 4 + 1) * P], xg_l[:, k * P:(k + 1) * P], ident)
                for k in range(KD):
                    tr = pe.transpose(ps[:, 6, k * CAP_C:(k + 1) * CAP_C], xg_c[:, k * P:(k + 1) * P], id16)
                tr.then_inc(xg_turned, 1)

            def unit(e, j, src):
                pe.wait_ge(wq_in[j], 16 * (e + 1))
                for m in range(2):
                    for k in range(KD):
                        mm = pe.matmul(ps[:, j % 4, m * CAP:(m + 1) * CAP], wq[j][:, k, m * P:(m + 1) * P], src[:, k, :],
                                       start=(k == 0), stop=(k == KD - 1))
                mm.then_inc(unit_made, 1)

            def expert(e, last):
                pe.wait_ge(xT_ready, 2 * e + 2)
                for j in range(8):
                    if j < 4:
                        pe.wait_ge(unit_act, 8 * e)
                    elif j % 2:
                        pe.wait_ge(unit_dve, 4 * e + (j - 3) // 2)
                    else:
                        pe.wait_ge(unit_act, 8 * e + (j - 2) // 2)
                    unit(e, j, xT)
                if not last:
                    pe.wait_ge(out_ready, 2 * e)
                    turn_rows(e + 1)
                pe.wait_ge(unit_act, 8 * e + 4)
                pe.wait_ge(unit_dve, 4 * e + 4)
                for j in range(8, 12):
                    unit(e, j, hid)
                pe.wait_ge(unit_act, 8 * e + 8)
                if not last:
                    pe.wait_ge(xT_ready, 2 * e + 4)
                else:
                    pe.wait_ge(out_ready, 2 * e)
                for k in range(KD):
                    pe.transpose(ps[:, 4 + k // 4, (k % 4) * P:(k % 4 + 1) * P], outT[:, k, 0:CAP_L], ident)
                for k in range(KD):
                    tr = pe.transpose(ps[0:CAP_C, 6 + k // 4, (k % 4) * P:(k % 4 + 1) * P], outT[:, k, CAP_L:CAP], ident)
                tr.then_inc(out_turned, 1)

            pe.wait_ge(affT_ready, 1)
            pe.wait_ge(sel_read, 4)
            turn_rows(0)
            with pe.Fori(0, EXPERTS - 1) as e:
                expert(e, False)
            expert(EXPERTS - 1, True)

        @block.scalar
        def _(act):
            steps = Steps(act, act_step)
            did, settle = steps.did, steps.settle

            act.wait_ge(vec_turned, 1)
            act.copy(vecT[:], ps[:, 6, 0:P]).then_inc(vec_ready, 1)
            act.wait_ge(vec_ready, 1)
            did(act.activation(cond[:, :, 0], vecT[:, V_CCTX:V_CCTX + KD], ACT.Silu))
            act.activation(cond[:, :, 1], vecT[:, V_C:V_C + KD], ACT.Silu).then_inc(cond_ready, 1)

            act.wait_ge(lg_part, 1)
            act.activation(lgt[:, 1], lgt[:, 1], ACT.Exp).then_inc(lg_exp, 1)
            act.wait_ge(lg_ready, 1)
            for h in range(HEADS):
                did(act.activation(decay[:, h, :], fwd, ACT.Exp, scale=lg[:, 0, h:h + 1]))
                did(act.activation(e2[:, h, :], bwd, ACT.Exp, scale=lg[:, 1, h:h + 1]))
                did(act.activation(xi[:, h, :], xarg, ACT.Exp, scale=lg[:, 2, h:h + 1]))
            did(act.activation(zeta[:, 0, :], lg[:, 0, :], ACT.Exp, scale=pos[:, 0:1]))
            did(act.activation(zeta[:, 1, :], lg[:, 1, :], ACT.Exp, scale=pos[:, 1:2]))
            act.activation(gchunk[:], lg[:, 2, :], ACT.Exp, scale=pos[:, 2:3]).then_inc(exp_ready, 1)

            def norm_x(n, b, k):
                act.wait_ge(x_in_s[b], k)
                act.wait_ge(ss_done, n)
                act.activation(sq[:], x_in[b][:].rearrange("p k n -> p (k n)"), ACT.Square, scale=D ** -0.5,
                               accum_out=stats[:, b:b + 1]).then_inc(ss_done, 1)
                act.wait_ge(rstd_done, n + 1)
                act.wait_ge(ss_done, n + 1)
                act.activation(x_in[b][:], x_in[b][:], ACT.Copy, scale=stats[:, 2 + b:3 + b]).then_inc(x_norm, 1)

            def high_h(n):
                act.wait_ge(x_mod, n + 1)
                plain(act)
                act.copy(h_hi[:, :, bass.ds(n * P, P)], hf[:]).then_inc(h_hi_done, 1)

            norm_x(0, 0, 16)
            with act.Fori(0, 4) as i:
                norm_x(2 * i + 1, 1, 16 * (i + 1))
                high_h(2 * i)
                norm_x(2 * i + 2, 0, 16 * (i + 2))
                high_h(2 * i + 1)
            high_h(8)

            def split(t0, per, i, c_):
                act.wait_ge(w_in_s[c_ % 2], 16 * ((t0 + c_) // 2 + 1) + 16 * (per // 2) * i)
                if t0 + c_ >= 2:
                    act.wait_ge(projected, t0 + c_ - 1 + per * i)
                act.copy(w_hi[:, c_ % 2], w_raw[:, c_ % 2]).then_inc(w_hi_done, 1)

            def out_of(slot):
                return ps[:, 3 * slot:3 * slot + NB, 0:CB]

            def evict(t, slot, dst, func, scale=1.0):
                act.wait_ge(projected, t + 1)
                plain(act)
                act.activation(dst.rearrange("p (b n) -> p b n", b=NB), out_of(slot), func, scale=scale)\
                   .then_inc(act_evicted, 1)

            def flat(t):
                return t[:].rearrange("p t n -> p (t n)")

            act.wait_ge(x_turned, NT)
            split(0, 6, 0, 0)
            act.wait_ge(exp_ready, 1)
            with steps.loop(PAIRS, 10) as i:
                def att(name, read):
                    for x in range(3):
                        b = ATT_AT[name, x]
                        act.wait_ge(att_made, N_ATT * i + b + 1)
                        plain(act)
                        read(x, ps[:, 6 + b % 2, 0:P * len(CHUNKS[x])].rearrange("p (t n) -> p t n", n=P)).then_inc(att_act, 1)

                def key_weights(x, src):
                    ts = slice(CHUNKS[x][0], CHUNKS[x][-1] + 1)
                    for h in range(2):
                        for d in range(2):
                            ins = act.activation(kz[h][:, ts, d * DK:(d + 1) * DK], src[:, :, h * DK:(h + 1) * DK], ACT.Copy,
                                                 scale=zeta2[:, d, h:h + 1])
                            if h + d < 2:
                                did(ins)
                    return ins

                def values(x, src):
                    return act.copy(v_tok[:, CHUNKS[x][0]:CHUNKS[x][-1] + 1, :], src)

                def z_of(h):
                    return z_ret[:, bass.ds(2 * i + h, 1), :].rearrange("p a t -> p (a t)")

                did(act.copy(zeta2[:], zeta[:, :, bass.ds(2 * i, 2)]))
                settle()
                split(0, 6, i, 1)
                evict(6 * i, 0, flat(qT), ACT.Copy)
                split(0, 6, i, 2)
                evict(6 * i + 1, 1, flat(kT), ACT.Copy, scale=DK ** -0.5)
                split(0, 6, i, 3)
                evict(6 * i + 2, 0, flat(vT), ACT.Copy)
                split(0, 6, i, 4)
                evict(6 * i + 3, 1, z_of(0), ACT.Silu)
                att("k_tok", key_weights)
                att("v_tok0", values)
                split(0, 6, i, 5)
                evict(6 * i + 4, 0, flat(vT), ACT.Copy)
                split(0, 6, i, 6)
                evict(6 * i + 5, 1, z_of(1), ACT.Silu)
                att("v_tok1", values)

            act.wait_ge(att_dve, N_ATT_BY["D"] * PAIRS)
            for k in range(KD):
                act.copy(z_hi[:, k, :], z_ret[:, k, :]).then_inc(z_hi_done, 1)
            with act.Fori(0, KD) as n:
                split(T_RETOUT, 2, n, 1)
                act.wait_ge(dve_evicted, ED_RETOUT + n)
                evict(T_RETOUT + 2 * n, 0, gate[:], ACT.Sigmoid)
                split(T_RETOUT, 2, n, 2)
            with act.Fori(0, KD // 2) as i:
                for s in range(2):
                    j = 2 * i + s
                    split(T_CONV, 6, i, 3 * s + 1)
                    act.wait_ge(conv_z, j)
                    if s == 0:
                        act.wait_ge(merged_stored, 16 * KD)
                    evict(T_CONV + 3 * j, s, cbT[:], ACT.Copy)
                    split(T_CONV, 6, i, 3 * s + 2)
                    evict(T_CONV + 3 * j + 1, 1 - s, ccT[:], ACT.Copy)
                    split(T_CONV, 6, i, 3 * s + 3)
                    act.wait_ge(conv_z_raw, j + 1)
                    plain(act)
                    act.copy(z_hi[:, bass.ds(j, 1), :].rearrange("p a t -> p (a t)"), ccT[:]).then_inc(z_hi_done, 1)

            def gate_out(n, last):
                split(T_CONVOUT, 2, n, 1)
                act.wait_ge(dve_evicted, ED_CONVOUT + n)
                act.wait_ge(conv_z, KD)
                evict(T_CONVOUT + 2 * n, 0, gate[:], ACT.Sigmoid)
                if not last:
                    split(T_CONVOUT, 2, n, 2)

            with act.Fori(0, KD - 1) as n:
                gate_out(n, False)
            gate_out(KD - 1, True)

            act.wait_ge(projected, T_WO - 1)
            for k in range(KD):
                act.wait_ge(w_in_s[k % 2], 16 * ((T_WO + k) // 2 + 1))
                act.copy(wo_hi[:, k, :], w_raw[:, k % 2].rearrange("p k n -> p (k n)")).then_inc(wo_hi_done, 1)

            def high_m(n, b, landed):
                act.wait_ge(m_in[b], landed)
                if not (isinstance(n, int) and n < 2):
                    act.wait_ge(m_made, n - 1)
                act.copy(m_hi[b][:], m_raw[b][:]).then_inc(m_hi_done, 1)

            def square_m(n, b):
                act.wait_ge(m_made, n + 1)
                act.wait_ge(x1_sq, n)
                act.activation(sq2[:].rearrange("p (a n) -> p a n", a=2), ps[:, 2 * b:2 * b + 2, :], ACT.Square, scale=D ** -0.5,
                               accum_out=stats[:, 4 + b:5 + b]).then_inc(m_sq, 1)

            def square_x1(n, b):
                act.wait_ge(x1_ready, n + 1)
                act.wait_ge(m_sq, n + 1)
                act.activation(sq2[:], x1[b][:], ACT.Square, scale=D ** -0.5, accum_out=stats[:, 6 + b:7 + b]).then_inc(x1_sq, 1)

            def h2_features(n):
                act.wait_ge(h2_turned, n + 1)
                if not isinstance(n, int) or n:
                    act.wait_ge(logit_made, n)
                act.copy(h2T[:].rearrange("p (a k) n -> p a (k n)", a=2), ps[:, 4:6, :]).then_inc(h2T_ready, 1)

            def exp_logits(n):
                act.wait_ge(logit_max, n + 1)
                plain(act)
                act.activation(aff[:, bass.ds(n, 1), :].rearrange("p a e -> p (a e)"), ps[:, 6, 0:EXPERTS], ACT.Exp,
                               bias=stats[:, 10:11], accum_out=stats[:, 11:12]).then_inc(logit_exp, 1)

            act.wait_ge(projected, T_WO)
            high_m(0, 0, 16)
            high_m(1, 1, 16)
            square_m(0, 0)
            square_x1(0, 0)

            def mix_step(n, b, landed):
                h2_features(n - 1)
                if landed is not None:
                    high_m(n + 1, b, landed)
                exp_logits(n - 1)
                square_m(n, 1 - b)
                square_x1(n, 1 - b)

            with act.Fori(0, 3) as i:
                mix_step(2 * i + 1, 0, 16 * (i + 2))
                mix_step(2 * i + 2, 1, 16 * (i + 2))
            mix_step(7, 0, 16 * 5)
            mix_step(8, 1, None)
            h2_features(8)
            exp_logits(8)

            def rows_to_xT(e):
                act.wait_ge(xg_turned, e + 1)
                act.copy(xT[:, :, 0:CAP_L], ps[:, 4:6, :].rearrange("p a (k n) -> p (a k) n", n=P)).then_inc(xT_ready, 1)
                act.copy(xT[:, :, CAP_L:CAP], ps[:, 6, 0:KD * CAP_C].rearrange("p (k n) -> p k n", n=CAP_C)).then_inc(xT_ready, 1)

            def unit_of(j):
                return ps[:, j % 4, 0:2 * CAP].rearrange("p (m n) -> p m n", m=2)

            def expert(e, last):
                for q in range(4):
                    act.wait_ge(unit_made, 12 * e + 2 * q + 1)
                    act.wait_ge(unit_dve, 4 * e + q)
                    act.activation(sg[:], unit_of(2 * q), ACT.Silu).then_inc(unit_act, 1)
                if not last:
                    rows_to_xT(e + 1)
                act.wait_ge(out_turned, e)
                for q in range(4):
                    act.wait_ge(unit_made, 12 * e + 9 + q)
                    act.copy(outT[:, 2 * q:2 * q + 2, :], unit_of(8 + q)).then_inc(unit_act, 1)

            rows_to_xT(0)
            with act.Fori(0, EXPERTS - 1) as e:
                expert(e, False)
            expert(EXPERTS - 1, True)

            def square_f(n, b, landed):
                act.wait_ge(f_in_s[b], landed)
                act.wait_ge(f_sq, n)
                act.activation(sq3[:], f_in[b][:], ACT.Square, scale=D ** -0.5, accum_out=stats[:, 16 + b:17 + b]).then_inc(f_sq, 1)

            square_f(0, 0, 16)
            with act.Fori(0, 4) as i:
                square_f(2 * i + 1, 1, 16 * (i + 1))
                square_f(2 * i + 2, 0, 16 * (i + 2))

        @block.vector
        def _(dve):
            steps = Steps(dve, dve_step)
            did, settle = steps.did, steps.settle

            def over(t, n):
                return t.unsqueeze(1).broadcast_to([P, n, t.shape[-1]])

            def along(t, n):
                return t.unsqueeze(2).broadcast_to([P, t.shape[1], n])

            dve.wait_ge(dec_in, 64)
            dve.scalar_tensor_tensor(lgt[:, 1], lgt[:, 0], -1.0, lgt[:, 0], ALU.mult, ALU.min).then_inc(lg_part, 1)
            did(dve.tensor_scalar(lg[:], lgt[:, 0], 0.0, None, ALU.min))
            dve.wait_ge(lg_exp, 1)
            e_, s_, s2, acc = lgt[:, 1], lgt[:, 2], lgt[:, 3], lgt[:, 4]
            did(dve.tensor_scalar(s_, e_, 2.0, None, ALU.add))
            settle()
            did(dve.reciprocal(s_, s_))
            settle()
            did(dve.tensor_tensor(s_, s_, e_, ALU.mult))
            settle()
            did(dve.tensor_tensor(s2, s_, s_, ALU.mult))
            settle()
            did(dve.tensor_scalar(acc, s2, 1.0 / 19, None, ALU.mult))
            for n in (17, 15, 13, 11, 9, 7, 5, 3):
                settle()
                did(dve.scalar_tensor_tensor(acc, acc, 1.0 / n, s2, ALU.add, ALU.mult))
            settle()
            did(dve.scalar_tensor_tensor(acc, acc, 1.0, s_, ALU.add, ALU.mult))
            settle()
            dve.scalar_tensor_tensor(lg[:], acc, -2.0, lg[:], ALU.mult, ALU.add).then_inc(lg_ready, 1)

            def read_ada(j):
                dve.wait_ge(ada_done, j + 1)
                dve.tensor_tensor(modT[:, KD * j:KD * j + KD, :], ps[:, j, 0:2 * KD].rearrange("p (k w) -> p k w", w=2),
                                  along(vecT[:, V_BADA + KD * j:V_BADA + KD * j + KD], 2), ALU.add).then_inc(ada_read, 1)

            dve.wait_ge(vec_ready, 1)
            read_ada(0)
            read_ada(1)
            dve.wait_ge(ada_read, 2)
            did(dve.scalar_tensor_tensor(scale1[:], modT[:, KD:2 * KD, :], 1.0,
                                         along(vecT[:, V_PREMIX:V_PREMIX + KD], 2), ALU.add, ALU.mult))
            settle()

            def modulate_x(n, which):
                dve.wait_ge(x_turned, n + 1)
                dve.wait_ge(h_hi_done, n)
                dve.wait_ge(h_lo_done, n)
                did(dve.tensor_tensor(hf[:], ps[:, 6:8, :].rearrange("p a (k n) -> p (a k) n", n=P),
                                      along(scale1[:, :, which], P), ALU.mult))
                settle()
                dve.tensor_tensor(hf[:], hf[:], along(modT[:, 0:KD, which], P), ALU.add).then_inc(x_mod, 1)

            def low_h(n):
                dve.wait_ge(h_hi_done, n + 1)
                dve.wait_ge(x_mod, n + 1)
                at_ = bass.ds(n * P, P)
                dve.tensor_tensor(h_lo[:, :, at_], hf[:], h_hi[:, :, at_].bitcast(F32), ALU.subtract).then_inc(h_lo_done, 1)

            modulate_x(0, 0)
            with steps.loop(3, 2) as i:
                for b in range(2):
                    low_h(2 * i + b)
                    modulate_x(2 * i + 1 + b, 1)
            low_h(6)
            modulate_x(7, 1)
            low_h(7)
            modulate_x(8, 1)
            low_h(8)

            for j in range(2, 6):
                read_ada(j)
            dve.wait_ge(ada_read, 6)
            for w_ in range(2):
                for table, chunk, vec in ((R_G1, 2, V_POSTMIX), (R_A2, 4, V_PREFFN), (R_SH2, 3, None), (R_G2, 5, V_POSTFFN)):
                    dst = rowsT[:, (2 * table + w_) * KD:(2 * table + w_ + 1) * KD]
                    src = modT[:, KD * chunk:KD * chunk + KD, w_]
                    if vec is None:
                        ins = dve.tensor_copy(dst, src)
                    else:
                        ins = dve.scalar_tensor_tensor(dst, src, 1.0 if table == R_A2 else 0.0, vecT[:, vec:vec + KD], ALU.add, ALU.mult)
                    if w_ == 1 and table == R_G2:
                        ins.then_inc(rows_made, 1)
                    else:
                        did(ins)
            dve.wait_ge(rows_turned, 1)
            dve.tensor_copy(rows[:], ps[0:64, 6, 0:P]).then_inc(rows_ready, 1)

            dve.wait_ge(exp_ready, 1)
            did(dve.tensor_tensor(decay[:], decay[:], over(mfwd, HEADS), ALU.mult))
            did(dve.tensor_tensor(e2[:], e2[:], over(mbwd, HEADS), ALU.mult))
            settle()
            did(dve.tensor_tensor(decay[:], decay[:], e2[:], ALU.add))
            settle()

            def split(t0, per, i, c_):
                dve.wait_ge(w_hi_done, t0 + per * i + c_ + 1)
                dve.tensor_tensor(w_lo[:, c_ % 2], w_raw[:, c_ % 2], w_hi[:, c_ % 2].bitcast(F32), ALU.subtract)\
                   .then_inc(w_lo_done, 1)

            def tiles(t):
                return t.rearrange("p (t n) -> p t n", n=P)

            split(0, 6, 0, 0)
            dve.wait_ge(rope_in, 16)
            dve.wait_ge(s0_in, 32)
            dve.wait_ge(rows_stored, 16)
            with steps.loop(PAIRS, 76) as i:
                def made(name, x):
                    dve.wait_ge(att_made, N_ATT * i + ATT_AT[name, x] + 1)

                def own(name, x):
                    dve.wait_ge(att_dve, N_ATT_BY["D"] * i + att_reads(name, x))

                def read(name, x, n=None):
                    b = 6 + ATT_AT[name, x] % 2
                    return ps[:, b, 0:(n or P * len(CHUNKS[x]))].rearrange("p (t n) -> p t n", n=P)

                def span(x):
                    return slice(CHUNKS[x][0], CHUNKS[x][-1] + 1)

                def rotate(name, dst, nth):
                    for x in range(2):
                        made(name, x)
                        dve.tensor_tensor(tiles(tmp[:, 512 * x:512 * x + 512]), read(name, x, 512),
                                          tiles(rope[:, 1, 512 * x:512 * x + 512]), ALU.mult).then_inc(att_dve, 1)
                    did(dve.tensor_tensor(dst[:, 1:NT, :], dst[:, 1:NT, :], tiles(rope[:, 0, :]), ALU.mult))
                    settle()
                    own(name, 1)
                    dve.tensor_tensor(dst[:, 1:NT, :], dst[:, 1:NT, :], tiles(tmp[:]), ALU.add).then_inc(roped, 1)
                    dve.wait_ge(roped, 2 * i + nth)

                def duplicate(h):
                    for x in range(2):
                        made(f"dup{h}", x)
                        dve.tensor_tensor(qx[:, 4 * x:4 * x + 4, :], read(f"dup{h}", x, 512),
                                          xi[:, bass.ds(2 * i + h, 1), :].broadcast_to([P, 4, P]), ALU.mult).then_inc(att_dve, 1)

                def scores(h):
                    for x in range(3):
                        made(f"score{h}", x)
                        dve.tensor_tensor(sm[:, span(x), :], read(f"score{h}", x),
                                          decay[:, bass.ds(2 * i + h, 1), :].broadcast_to([P, len(CHUNKS[x]), P]),
                                          ALU.mult).then_inc(att_dve, 1)

                def states(h):
                    head = 2 * i + h
                    made(f"kv{h}", 0)
                    dve.wait_ge(state_stored, 32 * head)
                    dve.tensor_copy(state_out[:], ps[:, 6 + ATT_AT[f"kv{h}", 0] % 2, 0:P]).then_inc(state_ready, 1)
                    did(dve.tensor_copy(rs[DK:P, 7, :], s0[DK:P, bass.ds(head, 1), :].rearrange("p a e -> p (a e)")))
                    dve.tensor_copy(rs[0:DK, 0, :], s0[0:DK, bass.ds(head, 1), :].rearrange("p a e -> p (a e)")).then_inc(att_dve, 1)
                    made(f"kv{h}", 2)
                    own(f"kv{h}", 0)

                    def update(part, src, dst):
                        b = 6 + ATT_AT[f"kv{h}", 1 + src // 4] % 2
                        return dve.scalar_tensor_tensor(rs[part, dst, :], rs[part, src, :], gchunk[part, bass.ds(head, 1)],
                                                        ps[part, b, (src % 4) * P:(src % 4 + 1) * P], ALU.mult, ALU.add)
                    for s in range(6):
                        settle()
                        did(update(slice(0, DK), s, s + 1))
                        did(update(slice(DK, P), 7 - s, 6 - s))
                    settle()
                    update(slice(DK, P), 1, 0).then_inc(att_dve, 1)
                    update(slice(0, DK), 6, 7).then_inc(att_dve, 1)

                def normalise(h):
                    for x in range(3):
                        made(f"o{h}", x)
                        src = read(f"o{h}", x)
                        for s, t in enumerate(CHUNKS[x]):
                            did(dve.bn_stats(gn6[:, t, :], src[:, s, :]))
                        settle()
                        did(dve.memset(stats[:, 30:31], 0.0))
                        for t in CHUNKS[x]:
                            ins = dve.bn_aggr(gnmv[:, t, :], gn6[:, t, :])
                            if t == CHUNKS[x][-1]:
                                ins.then_inc(gn_var, 1)
                            else:
                                did(ins)
                        dve.wait_ge(gn_rstd, 6 * i + 3 * h + x + 1)
                        for s, t in enumerate(CHUNKS[x]):
                            ins = dve.tensor_scalar(on[:, t, :], src[:, s, :], gnmv[:, t, 0:1], gnr[:, t:t + 1],
                                                    ALU.subtract, ALU.mult)
                            if t == CHUNKS[x][-1]:
                                ins.then_inc(att_dve, 1)
                            else:
                                did(ins)

                def gated(h):
                    dve.wait_ge(act_evicted, 6 * i + 4 + 2 * h)
                    for x in range(3):
                        made(f"o_feat{h}", x)
                        z = z_ret[:, bass.ds(2 * i + h, 1), P * CHUNKS[x][0]:P * CHUNKS[x][-1] + P].rearrange("p a t -> p (a t)")
                        dve.scalar_tensor_tensor(z, ps[:, 6 + ATT_AT[f"o_feat{h}", x] % 2, 0:P * len(CHUNKS[x])],
                                                 vecT[:, bass.ds(V_GN + 2 * i + h, 1)], z, ALU.mult, ALU.mult).then_inc(att_dve, 1)

                split(0, 6, i, 1)
                split(0, 6, i, 2)
                split(0, 6, i, 3)
                rotate("swap_q", qT, 1)
                rotate("swap_k", kT, 2)
                split(0, 6, i, 4)
                duplicate(0)
                split(0, 6, i, 5)
                scores(0)
                states(0)
                split(0, 6, i, 6)
                normalise(0)
                duplicate(1)
                gated(0)
                scores(1)
                states(1)
                normalise(1)
                gated(1)

            for k in range(KD):
                dve.wait_ge(z_hi_done, k + 1)
                dve.tensor_tensor(z_lo[:, k, :], z_ret[:, k, :], z_hi[:, k, :].bitcast(F32), ALU.subtract).then_inc(z_lo_done, 1)

            def banks(t):
                return t[:].rearrange("p (b n) -> p b n", b=NB)

            with dve.Fori(0, KD) as n:
                split(T_RETOUT, 2, n, 1)
                split(T_RETOUT, 2, n, 2)
                dve.wait_ge(projected, T_RETOUT + 2 * n + 2)
                dve.wait_ge(act_evicted, EA_RETOUT + n + 1)
                dve.wait_ge(merged_stored, 16 * n)
                dve.tensor_tensor(banks(merged), ps[:, 3:6, 0:CB], banks(gate), ALU.mult).then_inc(dve_evicted, 1)

            for x in (0, CTX + 1, TOK + 2):
                did(dve.memset(prod[:, x:x + 1], 0.0))
            with steps.loop(KD // 2, 12) as i:
                for s in range(2):
                    j = 2 * i + s
                    for c_ in range(3):
                        split(T_CONV, 6, i, 3 * s + c_ + 1)
                    dve.wait_ge(projected, T_CONV + 3 * j + 3)
                    dve.wait_ge(act_evicted, EA_CONV + 2 * j + 2)
                    b0 = 3 * s
                    did(dve.tensor_tensor(prod[:, 1:1 + CTX], ps[:, b0, 0:CTX], ccT[:, 0:CTX], ALU.mult))
                    did(dve.tensor_tensor(prod[:, CTX + 2:CB + 2], ps[:, b0, CTX:CB], ccT[:, CTX:CB], ALU.mult))
                    dve.tensor_tensor(prod[:, CB + 2:TOK + 2].rearrange("p (b n) -> p b n", n=CB), ps[:, b0 + 1:b0 + 3, 0:CB],
                                      ccT[:, CB:TOK].rearrange("p (b n) -> p b n", n=CB), ALU.mult).then_inc(dve_evicted, 1)
                    dve.wait_ge(dve_evicted, ED_CONV + j + 1)
                    settle()
                    did(dve.tensor_scalar(u[:, 0:TOK + 1], prod[:, 0:TOK + 1], vecT[:, bass.ds(V_CONV + j, 1)], None, ALU.mult))
                    for tap in (1, 2):
                        settle()
                        did(dve.scalar_tensor_tensor(u[:, 0:TOK + 1], prod[:, tap:TOK + 1 + tap],
                                                     vecT[:, bass.ds(V_CONV + KD * tap + j, 1)], u[:, 0:TOK + 1], ALU.mult, ALU.add))
                    settle()
                    did(dve.tensor_tensor(ccT[:, 0:CTX], cbT[:, 0:CTX], u[:, 0:CTX], ALU.mult))
                    dve.tensor_tensor(ccT[:, CTX:TOK], cbT[:, CTX:TOK], u[:, CTX + 1:TOK + 1], ALU.mult).then_inc(conv_z_raw, 1)
                    dve.wait_ge(conv_z_raw, j + 1)
                    dve.wait_ge(z_hi_done, KD + j + 1)
                    dve.tensor_tensor(z_lo[:, bass.ds(j, 1), :].rearrange("p a t -> p (a t)"), ccT[:],
                                      z_hi[:, bass.ds(j, 1), :].rearrange("p a t -> p (a t)").bitcast(F32), ALU.subtract)\
                       .then_inc(conv_z, 1)

            def merge(n, last):
                split(T_CONVOUT, 2, n, 1)
                if not last:
                    split(T_CONVOUT, 2, n, 2)
                dve.wait_ge(projected, T_CONVOUT + 2 * n + 2)
                dve.wait_ge(act_evicted, EA_CONVOUT + n + 1)
                dve.wait_ge(merged_stored, 16 * (KD + n))
                dve.tensor_tensor(banks(merged), ps[:, 3:6, 0:CB], banks(gate), ALU.mult).then_inc(dve_evicted, 1)
                dve.wait_ge(dve_evicted, ED_CONVOUT + n + 1)
                dve.wait_ge(ret_part_in, 16 * (n + 1))
                dve.tensor_tensor(merged[:], merged[:], ret_part[:], ALU.add).then_inc(merged_ready, 1)

            with dve.Fori(0, KD - 1) as n:
                merge(n, False)
            merge(KD - 1, True)

            for k in range(KD):
                dve.wait_ge(wo_hi_done, k + 1)
                dve.tensor_tensor(wo_lo[:, k, :], w_raw[:, k % 2].rearrange("p k n -> p (k n)"), wo_hi[:, k, :].bitcast(F32),
                                  ALU.subtract).then_inc(wo_lo_done, 1)

            def low_m(n, b):
                dve.wait_ge(m_hi_done, n + 1)
                dve.tensor_tensor(m_lo[b][:], m_raw[b][:], m_hi[b][:].bitcast(F32), ALU.subtract).then_inc(m_lo_done, 1)

            def residual(n, b, w_, landed):
                dve.wait_ge(m_rstd, n + 1)
                if not (isinstance(n, int) and n < 2):
                    dve.wait_ge(x1_stored[b], landed - 16)
                    dve.wait_ge(x1_sq, n - 1)
                did(dve.scalar_tensor_tensor(x1[b][:].rearrange("p (a n) -> p a n", a=2), ps[:, 2 * b:2 * b + 2, :],
                                             stats[:, 8 + b:9 + b], tabs[:, R_G1 * 2 + w_, :].rearrange("p (a n) -> p a n", a=2),
                                             ALU.mult, ALU.mult))
                dve.wait_ge(xr_in[b], landed)
                settle()
                dve.tensor_tensor(x1[b][:], x1[b][:], x_res[b][:], ALU.add).then_inc(x1_ready, 1)

            def ffn_input(n, b, w_, landed):
                dve.wait_ge(x1_rstd, n + 1)
                if not (isinstance(n, int) and n < 2):
                    dve.wait_ge(h2_stored[b], landed - 16)
                    dve.wait_ge(h2_turned, n - 1)
                did(dve.scalar_tensor_tensor(h2[b][:], x1[b][:], stats[:, 12 + b:13 + b], tabs[:, R_A2 * 2 + w_, :], ALU.mult, ALU.mult))
                settle()
                dve.tensor_tensor(h2[b][:], h2[b][:], tabs[:, R_SH2 * 2 + w_, :], ALU.add).then_inc(h2_ready, 1)

            def softmax(n):
                a = aff[:, bass.ds(n, 1), :].rearrange("p a e -> p (a e)")
                dve.wait_ge(logit_made, n + 1)
                did(dve.tensor_reduce(stats[:, 20:21], ps[:, 6, 0:EXPERTS], AX_X, ALU.max))
                settle()
                dve.tensor_scalar(stats[:, 10:11], stats[:, 20:21], -1.0, None, ALU.mult).then_inc(logit_max, 1)
                dve.wait_ge(logit_exp, n + 1)
                did(dve.reciprocal(stats[:, 21:22], stats[:, 11:12]))
                settle()
                dve.tensor_scalar(a, a, stats[:, 21:22], None, ALU.mult).then_inc(aff_done, 1)

            low_m(0, 0)
            low_m(1, 1)
            dve.wait_ge(tabs_in, 16 * 6)
            residual(0, 0, 0, 16)
            ffn_input(0, 0, 0, 16)

            def mix_step(n, b, landed, more):
                if more:
                    low_m(n + 1, b)
                softmax(n - 1)
                residual(n, 1 - b, 1, landed)
                ffn_input(n, 1 - b, 1, landed)

            mix_step(1, 0, 16, True)
            with steps.loop(3, 8) as i:
                mix_step(2 * i + 2, 1, 16 * (i + 2), True)
                mix_step(2 * i + 3, 0, 16 * (i + 2), True)
            mix_step(8, 1, 16 * 5, False)
            softmax(8)

            dve.wait_ge(aff_turned, 1)
            did(dve.tensor_copy(affT[:, 0:D].rearrange("p (a n) -> p a n", a=2), ps[0:EXPERTS, 0:2, :]))
            dve.tensor_copy(affT[:, D:TOK], ps[0:EXPERTS, 2, 0:P]).then_inc(affT_ready, 1)
            dve.wait_ge(affT_ready, 1)
            for pool_of, first, rounds in ((affT[:, 0:CTX], CAP_L, CAP_C // 8), (affT[:, CTX:TOK], 0, CAP_L // 8)):
                for r in range(rounds):
                    here = slice(first + 8 * r, first + 8 * r + 8)
                    settle()
                    did(dve.max(sel_v[:, here], pool_of))
                    settle()
                    did(dve.max_index(sel_i[:, here], sel_v[:, here], pool_of))
                    settle()
                    did(dve.match_replace(pool_of, sel_v[:, here], pool_of, -1.0))
            settle()
            dve.tensor_scalar(sel_f[:, 0:CAP_L], sel_i[:, 0:CAP_L], float(CTX), None, ALU.add).then_inc(sel_ready, 1)
            dve.tensor_copy(sel_f[:, CAP_L:CAP], sel_i[:, CAP_L:CAP]).then_inc(sel_ready, 1)
            dve.wait_ge(sel_turned, 1)
            dve.tensor_copy(idx_l[:], ps[:, 4, 32:32 + EXPERTS]).then_inc(sel_read, 1)
            dve.tensor_copy(idx_c[:], ps[0:CAP_C, 4, 48:48 + EXPERTS]).then_inc(sel_read, 1)
            dve.tensor_copy(val_l[:], ps[:, 4, 0:EXPERTS]).then_inc(sel_read, 1)
            dve.tensor_copy(val_c[:], ps[0:CAP_C, 4, 16:16 + EXPERTS]).then_inc(sel_read, 1)
            dve.wait_ge(sel_read, 4)

            with dve.Fori(0, EXPERTS) as e:
                for q in range(4):
                    dve.wait_ge(unit_made, 12 * e + 2 * q + 2)
                    dve.wait_ge(unit_act, 8 * e + q + 1)
                    dve.tensor_tensor(hid[:, 2 * q:2 * q + 2, :],
                                      ps[:, (2 * q + 1) % 4, 0:2 * CAP].rearrange("p (m n) -> p m n", m=2), sg[:], ALU.mult)\
                       .then_inc(unit_dve, 1)
                dve.wait_ge(out_turned, e + 1)
                dve.wait_ge(added_l, 16 * e)
                dve.wait_ge(added_c, 16 * e)
                dve.tensor_scalar(ot_l[:].rearrange("p (a n) -> p a n", a=2), ps[:, 4:6, :], val_l[:, bass.ds(e, 1)], None,
                                  ALU.mult).then_inc(out_ready, 1)
                dve.tensor_scalar(ot_c[:].rearrange("p (a n) -> p a n", a=2), ps[0:CAP_C, 6:8, :], val_c[:, bass.ds(e, 1)], None,
                                  ALU.mult).then_inc(out_ready, 1)

            def last_residual(n, b, w_, landed):
                dve.wait_ge(f_rstd, n + 1)
                if not (isinstance(n, int) and n < 2):
                    dve.wait_ge(y_stored[b], landed - 16)
                did(dve.scalar_tensor_tensor(y_out[b][:], f_in[b][:], stats[:, 18 + b:19 + b], g2[:, w_, :], ALU.mult, ALU.mult))
                dve.wait_ge(x1_in_s[b], landed)
                settle()
                dve.tensor_tensor(y_out[b][:], y_out[b][:], x1_in[b][:], ALU.add).then_inc(y_ready, 1)

            dve.wait_ge(g2_in, 32)
            last_residual(0, 0, 0, 16)
            last_residual(1, 1, 1, 16)
            with steps.loop(3, 2) as i:
                last_residual(2 * i + 2, 0, 1, 16 * (i + 2))
                last_residual(2 * i + 3, 1, 1, 16 * (i + 2))
            last_residual(8, 0, 1, 16 * 5)


_INS = ["x_prompt", "x_sample", "state_ret_fwd", "state_ret_bwd", "c", "c_ctx", "w_ada", "b_ada", "norm_pre_mix",
        "norm_post_mix", "norm_pre_ffn", "norm_post_ffn", "w_in", "ret_decay_fwd", "ret_decay_bwd", "ret_norm_g",
        "conv_w", "w_ret_o", "w_conv_o", "w_o", "w_router", "w_gate", "w_up", "w_down"]
_OUTS = [(1, CTX, D), (1, LAT, D), (1, 1, HEADS, DK, DV), (1, 1, HEADS, DK, DV)]


def kernel(**inputs):
    import concourse.bacc as _bacc
    from concourse.bass_utils import run_bass_kernel_spmd as _run

    nc = _bacc.Bacc("TRN2", target_bir_lowering=False, num_devices=1)
    arrays, args = {}, []
    for name in _INS:
        a = np.ascontiguousarray(inputs[name])
        arrays[f"in_{name}_dram"] = a
        args.append(nc.dram_tensor(f"in_{name}_dram", a.shape, F32, kind="ExternalInput").ap())
    small, rope = shape_tables()
    for name, a in (("small", small), ("rope", rope)):
        arrays[f"table_{name}_dram"] = np.ascontiguousarray(a)
        args.append(nc.dram_tensor(f"table_{name}_dram", a.shape, F32, kind="ExternalInput").ap())
    for i, shape in enumerate(_OUTS):
        args.append(nc.dram_tensor(f"out_{i}_dram", shape, F32, kind="ExternalOutput").ap())
    build(nc, *args)
    r = _run(nc, [arrays], core_ids=[0])
    return tuple(r.results[0][f"out_{i}_dram"] for i in range(len(_OUTS)))
```

```python
from contextlib import ExitStack, contextmanager

import concourse.bass as bass
from concourse import mybir
import numpy as np

ALU = mybir.AluOpType
ACT = mybir.ActivationFunctionType
F32 = mybir.dt.float32
F32R = mybir.dt.float32r
U32 = mybir.dt.uint32
AX_X = mybir.AxisListType.X

P = 128
D = 1024
KD = D // P
CTX, LAT = 128, 1024
TOK = CTX + LAT
NT = TOK // P
HEADS, DK, DV = 8, 64, 128
PAIRS = HEADS // 2
GRID_W = 64
NB = 3
CB = TOK // NB
EXPERTS = 16
CAP_L, CAP_C = 2 * LAT // EXPERTS, 2 * CTX // EXPERTS
CAP = CAP_L + CAP_C
HALF = LAT // 2
HALF_T = HALF // P
E2 = 2 * EXPERTS
RMS_EPS, GN_EPS = 1e-6, 1e-5

COL_Q, COL_K, COL_V, COL_G, COL_CB, COL_CC, COL_CX, COL_GA, COL_GB = 0, 4, 8, 16, 24, 32, 40, 48, 56

T_RET = 0
T_RETOUT = T_RET + 6 * PAIRS
T_CONV = T_RETOUT + 2 * KD
T_CONVOUT = T_CONV + 3 * KD
T_WO = T_CONVOUT + 2 * KD

EA_RETOUT, ED_RETOUT = 6 * PAIRS, 0
EA_CONV, ED_CONV = EA_RETOUT + KD, ED_RETOUT + KD
EA_CONVOUT, ED_CONVOUT = EA_CONV + 2 * KD, ED_CONV + KD

V_BADA, V_PREMIX, V_GN, V_CONV, N_VEC = 0, 16, 24, 32, 56
R_G1, R_SH2, R_A2, R_G2 = 0, 1, 2, 3

CHUNKS = [range(0, 1), range(1, 5), range(5, 9)]
ATT = ([("before", x, "D") for x in range(3)]
       + [("swap_q", x, "D") for x in range(2)] + [("swap_k", x, "D") for x in range(2)]
       + [("v_tok0", x, "A") for x in range(3)]
       + [("k_tok", x, "A") for x in range(3)] + [("dup0", x, "D") for x in range(2)]
       + [("score0", x, "D") for x in range(3)] + [("kv0", x, "D") for x in range(3)]
       + [("o0", x, "D") for x in range(3)]
       + [("v_tok1", x, "A") for x in range(3)] + [("dup1", x, "D") for x in range(2)]
       + [("score1", x, "D") for x in range(3)] + [("o_feat0", x, "D") for x in range(3)]
       + [("kv1", x, "D") for x in range(3)] + [("o1", x, "D") for x in range(3)])
ATT_AT = {(n, x): b for b, (n, x, _) in enumerate(ATT)}
N_ATT = len(ATT)
N_ATT_BY = {e: sum(a[2] == e for a in ATT) for e in "AD"}


def att_count(i, name, x):
    return N_ATT * i - 3 + ATT_AT[name, x] + 1


def att_reads(i, name, x):
    b = ATT_AT[name, x]
    who = ATT[b][2]
    return N_ATT_BY[who] * i - (3 if who == "D" else 0) + sum(a[2] == who for a in ATT[:b + 1])


READS_D, READS_A = N_ATT_BY["D"] * PAIRS, N_ATT_BY["A"] * PAIRS


def shape_tables():
    i = np.arange(P)
    f = np.float32
    ident = np.eye(P, dtype=f)
    partner = np.where(i % 32 < 16, i + 16, i - 16)
    swap = (i[:, None] == partner[None, :]).astype(f)
    dup = [(i[:, None] == 64 * h + i[None, :] % 64).astype(f) for h in range(2)]
    xarg = np.where(i[:, None] < DK, i[None, :] + 1, P - i[None, :]).astype(f)
    diff = (i[None, :] - i[:, None]).astype(f)
    fwd, bwd = np.maximum(diff, 0), np.maximum(-diff, 0)
    mfwd, mbwd = (diff >= 0).astype(f), (diff <= 0).astype(f)
    pos = np.stack([P - 1 - i, i, np.full(P, P)], 1).astype(f)
    inv = (f(10000.0) ** (-np.arange(16, dtype=f) / f(16))).astype(f)
    t = np.arange(LAT)
    where = np.where((i % 64 < 32)[:, None], (t // GRID_W)[None, :], (t % GRID_W)[None, :]).astype(f)
    ang = where * inv[i % 16][:, None]
    cos, sin = np.cos(ang).astype(f), np.sin(ang).astype(f)
    sin = np.where((i % 32 < 16)[:, None], -sin, sin)
    small = np.concatenate([ident, swap, dup[0], dup[1], xarg, fwd, bwd, mfwd, mbwd, pos, np.full((P, NT), -0.5, f), np.full((P, 4), GN_EPS, f),
                            np.full((P, NT), RMS_EPS, f), ident[::-1]], 1)
    return small.astype(f), np.stack([cos, sin], 1).astype(f)


N_SMALL = 9 * P + 3 + NT + 4 + NT


def parts_of(b):
    return [(0, slice(0, CTX)), (1, slice(CTX, CB))] if b == 0 else [(1, slice(b * CB, (b + 1) * CB))]


def each(eng, count, body):
    body(0)
    with eng.Fori(1, count) as i:
        body(i)


class Steps:

    def __init__(self, eng, sem):
        self.eng, self.sem, self.base, self.n = eng, sem, 0, 0

    def did(self, ins):
        ins.then_inc(self.sem, 1)
        self.n += 1

    def settle(self):
        self.eng.wait_ge(self.sem, self.base + self.n)

    @contextmanager
    def loop(self, count, per, start=0):
        with self.eng.Fori(start, count) as i:
            before = self.n
            self.base, self.n = before + (i - start) * per, 0
            yield i
            assert self.n == per, (self.n, per)
        self.base, self.n = 0, before + (count - start) * per

    def each(self, count, per, body):
        before = self.n
        body(0)
        assert self.n - before == per, (self.n - before, per)
        with self.loop(count, per, start=1) as i:
            body(i)

    def settle_but_last(self):
        self.eng.wait_ge(self.sem, self.base + self.n - 1)


def build(nc, x_prompt, x_sample, state_f, state_b, c, c_ctx, w_ada, b_ada, n_pre_mix, n_post_mix,
          n_pre_ffn, n_post_ffn, w_in, dec_f, dec_b, gn_g, conv_w, w_ret_o, w_conv_o, w_o, w_router,
          w_gate, w_up, w_down, small_tab, rope_tab, y_prompt, y_sample, new_f, new_b):
    with ExitStack() as ctx:
        BASE = 16512

        def at(name, offset, shape, dt=F32):
            return nc.alloc_sbuf_tensor_at(name, shape, dt, offset=BASE + offset)

        def sem(name):
            return ctx.enter_context(nc.semaphore(name))

        def dram(name, shape):
            return nc.dram_tensor(name, shape, F32, kind="Internal").ap()

        FT = TOK * 4
        SL = D * 4
        A_H = 0
        A_W = 2 * KD * FT
        A_ZA = A_W + 6 * SL
        A_ZB = A_ZA + KD * FT
        A_C = A_ZB + KD * FT
        h_hi = at("h_hi", A_H, [P, KD, TOK], F32R)
        h_lo = at("h_lo", A_H + KD * FT, [P, KD, TOK], F32R)
        w_hi = at("w_hi", A_W, [P, 2, KD, P], F32R)
        w_lo = at("w_lo", A_W + 2 * SL, [P, 2, KD, P], F32R)
        w_raw = at("w_raw", A_W + 4 * SL, [P, 2, KD, P])
        z_ret = at("z_ret", A_ZA, [P, HEADS, TOK])
        z_lo = at("z_lo", A_ZA, [P, KD, TOK], F32R)
        z_hi = at("z_hi", A_ZB, [P, KD, TOK], F32R)

        off = A_C
        def const(name, shape, dt=F32):
            nonlocal off
            size = 4
            for n in shape[1:]:
                size *= n
            t = at(name, off, shape, dt)
            off += (size + 31) // 32 * 32
            return t

        small = const("small", [P, N_SMALL])
        ident, swap = small[:, 0:P], small[:, P:2 * P]
        dup = [small[:, (2 + h) * P:(3 + h) * P] for h in range(2)]
        xarg = small[:, 4 * P:5 * P]
        fwd, bwd = small[:, 5 * P:6 * P], small[:, 6 * P:7 * P]
        mfwd, mbwd = small[:, 7 * P:8 * P], small[:, 8 * P:9 * P]
        pos = small[:, 9 * P:9 * P + 3]
        minus_half, gn_eps, rms_eps = (small[:, 9 * P + a:9 * P + b] for a, b in ((3, 3 + NT), (3 + NT, 7 + NT), (7 + NT, 7 + 2 * NT)))
        vecT = const("vecT", [P, N_VEC])
        modT = const("modT", [P, 16, 2])
        scale1 = const("scale1", [P, KD, 2])
        cond = const("cond", [P, KD, 2])
        lg = const("lg", [P, 3, HEADS])
        lgt = const("lgt", [P, 5, 3, HEADS])
        zeta = const("zeta", [P, 2, HEADS])
        zeta2 = const("zeta2", [P, 2, 2])
        gchunk = const("gchunk", [P, HEADS])
        decay = const("decay", [P, HEADS, P])
        xi = const("xi", [P, HEADS, P])
        stats = const("stats", [P, 64])
        x_ms, x_rstd = stats[:, 32:32 + NT], stats[:, 48:48 + NT]
        f_ms, f_rs = x_ms, x_rstd
        gn6 = const("gn6", [P, NT, 6])
        gnmv = const("gnmv", [P, NT, 2])
        gnr = const("gnr", [P, NT])
        state_out = const("state_out", [P, P])
        A_S = off
        rope = at("rope", A_S, [P, 2, LAT])

        names = ["qT", "kT", "kz0", "kz1", "vT", "v_tok", "sm", "on"]
        ret = {n: at(n, A_ZB + j * FT, [P, NT, P]) for j, n in enumerate(names)}
        qT, kT, v_tok, sm, on = ret["qT"], ret["kT"], ret["v_tok"], ret["sm"], ret["on"]
        vT = ret["vT"]
        kz = [ret["kz0"], ret["kz1"]]
        A_S2 = A_S + 2 * SL
        tmp = at("tmp", A_S2, [P, LAT])
        qx = at("qx", A_S2 + SL, [P, LAT // P, P])
        rs = at("rs", A_S2 + 2 * SL, [P, LAT // P, P])
        s0 = at("s0", A_S2 + 3 * SL, [P, HEADS, P])
        assert BASE + A_S2 + 4 * SL <= nc.sbuf_usable_end, (BASE + A_S2 + 4 * SL, nc.sbuf_usable_end)

        ada = [at(f"ada{j}", A_ZA + j * KD * 2048, [P, KD, 512]) for j in range(2)]
        vec_in = at("vec_in", A_ZA + 2 * KD * 2048, [N_VEC, P])
        c_in = at("c_in", A_ZA + 2 * KD * 2048 + 512, [2 * KD, P])
        xa = at("xa", A_ZB, [P, NT, D])
        xF = at("xF", A_H + KD * FT, [P, KD, TOK])
        e2 = at("e2", A_S2, [P, HEADS, P])
        mrow = at("mrow", A_S2 + SL, [2, 4, 512])
        sq = at("sq", A_W, [P, D])

        A_M = A_S + 2 * FT
        ada_k = [at(f"ada_k{j}", A_M + j * 2048, [P, 512]) for j in range(2)]
        ada_acc = at("ada_acc", A_M + 4096, [P, 2, 512])
        b_row = at("b_row", A_M + 8192, [1, 512])
        mod_row = at("mod_row", A_M + 10240, [1, 2, 512])

        gate = at("gate", A_S, [P, TOK])
        merged = at("merged", A_S + FT, [P, TOK])
        ret_part = at("ret_part", A_S + 2 * FT, [P, TOK])
        cbT = at("cbT", A_S, [P, TOK])
        ccT = at("ccT", A_S + FT, [P, TOK])
        prod = at("prod", A_S + 2 * FT, [P, TOK + 8])
        u = at("u", A_S + 3 * FT + 32, [P, TOK + 8])

        wo_hi = at("wo_hi", A_H, [P, KD, D], F32R)
        wo_lo = at("wo_lo", A_H + KD * SL, [P, KD, D], F32R)
        Z = A_ZA
        m_raw = [at(f"m_raw{j}", A_S + 3 * FT + j * SL, [P, KD, P]) for j in range(2)]
        wo_raw = [w_raw[:, 0], w_raw[:, 1]] + [at(f"wo_raw{j}", (16 + j) * SL, [P, KD, P])[:] for j in range(2)]
        m_hi = [at(f"m_hi{j}", A_W + j * SL, [P, KD, P], F32R) for j in range(2)]
        m_lo = [at(f"m_lo{j}", A_W + (2 + j) * SL, [P, KD, P], F32R) for j in range(2)]
        x_res = [at(f"x_res{j}", Z + (1 + j) * SL, [P, D]) for j in range(2)]
        norm_bc = at("norm_bc", Z + 3 * SL, [P, 2, D])
        tabs = at("tabs", Z + 8 * SL, [P, 6, D])
        x1 = [at(f"x1_{j}", Z + (14 + j) * SL, [P, D]) for j in range(2)]
        h2 = [at(f"h2_{j}", Z + (16 + j) * SL, [P, D]) for j in range(2)]
        h2T = at("h2T", A_S, [P, KD, P])
        sq2 = at("sq2", A_S + SL, [P, D])
        w_rt = at("w_rt", A_S + 2 * SL, [P, KD, EXPERTS])
        aff = at("aff", A_S + 2 * SL + 512, [P, 1 + HALF_T, 3, EXPERTS])
        flip = at("flip", A_S + SL, [P, P])
        affT = at("affT", A_S + 3 * SL, [E2 + EXPERTS, HALF + CTX])
        sel_v = at("sel_v", A_S + 3 * SL + FT, [E2 + EXPERTS, CAP])
        sel_i = at("sel_i", A_S + 3 * SL + FT + 576, [E2 + EXPERTS, CAP], U32)
        sel_f = at("sel_f", A_S + 3 * SL + FT + 1152, [E2 + EXPERTS, CAP])
        A_V = A_S + 2 * SL + 1472
        val_l = at("val_l", A_V, [P, EXPERTS])
        val_c = at("val_c", A_V + 64, [CAP_C, EXPERTS])
        idx_l = at("idx_l", A_V + 128, [P, EXPERTS], U32)
        idx_c = at("idx_c", A_V + 192, [CAP_C, EXPERTS], U32)
        halves = at("halves", A_V + 256, [P, 2, E2 + EXPERTS])

        wq = [at(f"wq{j}", j * 2 * SL, [P, KD, 2 * P]) for j in range(12)]
        xg_l = at("xg_l", Z, [P, D])
        xg_c = at("xg_c", Z + SL, [CAP_C, D])
        xT = at("xT", Z + 2 * SL, [P, KD, CAP])
        sg = at("sg", Z + 2 * SL + 4608, [P, 2, CAP])
        hid = at("hid", Z + 3 * SL + 4608, [P, KD, CAP])
        outT = at("outT", Z + 3 * SL + 2 * 4608, [P, KD, CAP])
        ot_l = at("ot_l", Z + 3 * SL + 3 * 4608, [P, D])
        ot_c = at("ot_c", Z + 4 * SL + 3 * 4608, [CAP_C, D])
        zero = at("zero", A_S, [P, D])
        g2 = at("g2", Z + 9 * SL, [P, 2, D])
        norm_ffn = at("norm_ffn", Z + 17 * SL, [P, D])
        sq3 = at("sq3", Z + 16 * SL, [P, D])
        x1_all = at("x1_all", 0, [P, NT, D])
        f_all = at("f_all", 10 * SL, [P, NT, D])
        y_all = at("y_all", Z, [P, NT, D])

        def aff_of(n):
            if isinstance(n, int) and n > HALF_T:
                return aff[:, n - HALF_T, 2, :]
            return aff[:, bass.ds(n, 1), 0:1, :].rearrange("p a b e -> p (a b e)")

        ps = ctx.enter_context(nc.psum_tensor("ps", [P, 8, 512], F32))

        mod_d = dram("mod_d", [2, 4 * D])
        merged_d = dram("merged_d", [KD, P, TOK])
        x1_d = dram("x1_d", [NT, P, D])
        h2_d = dram("h2_d", [TOK, D])
        ffn_d = dram("ffn_d", [TOK, D])

        xp = x_prompt[0]
        xs = x_sample[0].rearrange("(t p) d -> t p d", p=P)
        yp = y_prompt[0]
        ys = y_sample[0].rearrange("(t p) d -> t p d", p=P)

        def cols(w, j):
            return w[:, bass.ds(j * P, P)].rearrange("(k p) n -> p k n", p=P)

        small_in, vec_in_s, dec_in, rope_in, s0_in = (sem(n) for n in ("small_in", "vec_in_s", "dec_in", "rope_in", "s0_in"))
        ada_in = [sem(f"ada_in{j}") for j in range(2)]
        x_landed = sem("x_landed")
        w_in_s = [sem(f"w_landed{j}") for j in range(2)]
        act_step, dve_step, pool_step = sem("act_step"), sem("dve_step"), sem("pool_step")
        c_landed, c_turned = sem("c_landed"), sem("c_turned")
        vec_turned, vec_ready, cond_ready = sem("vec_turned"), sem("vec_ready"), sem("cond_ready")
        ada_done, mrow_ready, mod_turned = sem("ada_done"), sem("mrow_ready"), sem("mod_turned")
        ada_k_in = [sem(f"ada_k_in{j}") for j in range(2)]
        ada_used, ada_summed = sem("ada_used"), sem("ada_summed")
        b_row_in, mod_row_ready, mod_row_stored = sem("b_row_in"), sem("mod_row_ready"), sem("mod_row_stored")
        mod_read, scale_ready = sem("mod_read"), sem("scale_ready")
        norm_ffn_in, g2_ready = sem("norm_ffn_in"), sem("g2_ready")
        x_feat, x_feat_act = sem("x_feat"), sem("x_feat_act")
        x_norm, x_turned, h_hi_done, h_lo_done = (sem(n) for n in ("x_norm", "x_turned", "h_hi_done", "h_lo_done"))
        ss_done, rstd_done = sem("ss_done"), sem("rstd_done")
        lg_part, lg_exp, lg_ready, exp_ready = sem("lg_part"), sem("lg_exp"), sem("lg_ready"), sem("exp_ready")
        w_hi_done, w_lo_done, projected = sem("w_hi_done"), sem("w_lo_done"), sem("projected")
        act_evicted, dve_evicted = sem("act_evicted"), sem("dve_evicted")
        att_made, att_act, att_dve = sem("att_made"), sem("att_act"), sem("att_dve")
        roped, state_ready, state_stored = sem("roped"), sem("state_ready"), sem("state_stored")
        z_hi_done, z_lo_done = sem("z_hi_done"), sem("z_lo_done")
        merged_ready, merged_stored, ret_part_in = sem("merged_ready"), sem("merged_stored"), sem("ret_part_in")
        conv_z, conv_z_raw = sem("conv_z"), sem("conv_z_raw")
        wo_hi_done, wo_lo_done = sem("wo_hi_done"), sem("wo_lo_done")
        wo_in = [sem(f"wo_in{j}") for j in range(4)]
        m0_hi_most, m0_lo_most = sem("m0_hi_most"), sem("m0_lo_most")
        tabs_in, router_in = [sem("tabs_ctx_in"), sem("tabs_lat_in")], sem("router_in")
        m_in = [sem(f"m_in{j}") for j in range(2)]
        xr_in = [sem(f"xr_in{j}") for j in range(2)]
        m_hi_done, m_lo_done, m_made, m_sq = sem("m_hi_done"), sem("m_lo_done"), sem("m_made"), sem("m_sq")
        x1_ready, x1_sq, h2_ready = sem("x1_ready"), sem("x1_sq"), sem("h2_ready")
        x1_stored, h2_stored = ([sem(f"{n}{j}") for j in range(2)] for n in ("x1_stored", "h2_stored"))
        h2_turned, h2T_ready, logit_made, logit_max, logit_exp, aff_done = (
            sem(n) for n in ("h2_turned", "h2T_ready", "logit_made", "logit_max", "logit_exp", "aff_done"))
        aff_turned, affT_ready, sel_ready, sel_turned, sel_read = (
            sem(n) for n in ("aff_turned", "affT_ready", "sel_ready", "sel_turned", "sel_read"))
        flip_in, sel_copied, sel_flipped = sem("flip_in"), sem("sel_copied"), sem("sel_flipped")
        zero_ready, ffn_zeroed = sem("zero_ready"), sem("ffn_zeroed")
        wq_in = [sem(f"wq_in{j}") for j in range(12)]
        unit_made, unit_act, unit_dve = sem("unit_made"), sem("unit_act"), sem("unit_dve")
        got_l, got_c = sem("got_l"), sem("got_c")
        xg_turned, xT_ready, out_turned, out_ready = sem("xg_turned"), sem("xT_ready"), sem("out_turned"), sem("out_ready")
        added_l, added_c = sem("added_l"), sem("added_c")
        g2_in = sem("g2_in")
        x1_landed = sem("x1_landed")
        f_in_s = [sem(f"f_in_s{g}") for g in range(3)]
        f_sq, f_rstd, f_scaled = sem("f_sq"), sem("f_rstd"), sem("f_scaled")
        y_ready, y_stored = sem("y_ready"), sem("y_stored")
        m_rstd, x1_rstd, gn_var, gn_rstd = sem("m_rstd"), sem("x1_rstd"), sem("gn_var"), sem("gn_rstd")

        tally = {}

        def plain(eng):
            name = str(eng.engine).split(".")[-1]
            if name not in tally:
                tally[name] = eng.alloc_register(f"tally_{name}")
                eng.reg_mov(tally[name], 0)
            eng.reg_add(tally[name], tally[name], 1)

        block = ctx.enter_context(nc.Block())

        @block.sync
        def _(sp):
            for j, v in enumerate((c_ctx, c[0])):
                sp.dma_start(c_in[j * KD:(j + 1) * KD, :], v.rearrange("(r p) -> r p", p=P)).then_inc(c_landed, 16)
            sp.dma_start(small[:], small_tab[:, 0:N_SMALL]).then_inc(small_in, 16)

            def load_ada(j):
                if j >= 2:
                    sp.wait_ge(ada_done, j - 1)
                sp.dma_start(ada[j % 2][:], w_ada[0][:, 512 * j:512 * j + 512].rearrange("(k p) n -> p k n", p=P))\
                  .then_inc(ada_in[j % 2], 16)

            load_ada(0)
            sp.dma_start(xa[:, 0, :], xp).then_inc(x_landed, 16)
            sp.dma_start(xa[:, 1:NT, :], xs.rearrange("t p d -> p t d")).then_inc(x_landed, 16)
            for j in range(1, 4):
                load_ada(j)

            def load_w(i, t0, per, c_, src):
                sp.wait_ge(w_lo_done, t0 + per * i + c_ - 1)
                sp.dma_start(w_raw[:, c_ % 2], src).then_inc(w_in_s[c_ % 2], 16)

            w = w_in[0]
            sp.dma_start(rope[:], rope_tab).then_inc(rope_in, 16)
            def load_pair(i):
                for c_, col in enumerate((COL_Q + i, COL_K + i, COL_V + 2 * i, COL_V + 2 * i + 1,
                                          COL_G + 2 * i, COL_G + 2 * i + 1)):
                    if c_ == 0:
                        sp.wait_ge(w_lo_done, 6 * i)
                    elif c_ >= 2:
                        sp.wait_ge(w_lo_done, 6 * i + c_ - 1)
                    sp.dma_start(w_raw[:, c_ % 2], cols(w, col)).then_inc(w_in_s[c_ % 2], 16)
            each(sp, PAIRS, load_pair)

            def load_gates(i):
                load_w(i, T_RETOUT, 2, 0, cols(w, COL_GA + i))
                load_w(i, T_RETOUT, 2, 1, cols(w_ret_o[0], i))
                sp.wait_ge(att_dve, READS_D)
                for k in range(KD):
                    if k < 2:
                        sp.wait_ge(ada_used, 8 * i + k - 1) if k else sp.wait_ge(mod_row_ready, i)
                    else:
                        sp.wait_ge(ada_used, 8 * i + k - 1)
                    sp.dma_start(ada_k[k % 2][:], w_ada[0][k * P:(k + 1) * P, bass.ds(2 * D + 512 * i, 512)])\
                      .then_inc(ada_k_in[k % 2], 16)
                sp.dma_start(b_row[:], b_ada[0:1, bass.ds(2 * D + 512 * i, 512)]).then_inc(b_row_in, 16)
            each(sp, KD, load_gates)

            with sp.Fori(0, KD // 2) as i:
                for c_ in range(6):
                    load_w(i, T_CONV, 6, c_, cols(w, (COL_CB, COL_CC, COL_CX)[c_ % 3] + 2 * i + c_ // 3))
            with sp.Fori(0, KD) as i:
                load_w(i, T_CONVOUT, 2, 0, cols(w, COL_GB + i))
                load_w(i, T_CONVOUT, 2, 1, cols(w_conv_o[0], i))
            def load_wo(k):
                sp.dma_start(wo_raw[k % 4], w_o[0][k * P:(k + 1) * P, :].rearrange("p (k n) -> p k n", n=P)).then_inc(wo_in[k % 4], 16)

            sp.wait_ge(w_lo_done, T_WO - 1)
            load_wo(0)
            sp.wait_ge(merged_stored, 16 * (2 * KD - 1))
            for b in range(2):
                sp.dma_start(m_raw[b][:, 0:KD - 1, :], merged_d[0:KD - 1, :, b * P:(b + 1) * P].rearrange("k p n -> p k n"))\
                  .then_inc(m_in[b], 16)
            sp.wait_ge(w_lo_done, T_WO)
            load_wo(1)
            sp.wait_ge(projected, T_WO - 1)
            load_wo(2)
            load_wo(3)
            for k in range(4, KD):
                sp.wait_ge(wo_lo_done, k - 3)
                load_wo(k)

            sp.wait_ge(projected, T_WO)
            sp.wait_ge(mod_row_stored, 16 * KD)

            def load_tab(j, w_):
                sp.dma_start(tabs[:, 2 * j + w_, :], mod_d[w_:w_ + 1, j * D:(j + 1) * D].broadcast_to([P, D])).then_inc(tabs_in[w_], 16)

            def load_norm(j, v):
                sp.dma_start(norm_bc[:, j, :], v[0:1, :].broadcast_to([P, D])).then_inc(tabs_in[0], 16)

            sp.dma_start(x_res[0][:], xp).then_inc(xr_in[0], 16)
            load_tab(R_G1, 0)
            load_norm(0, n_post_mix)
            load_tab(R_A2, 0)
            load_norm(1, n_pre_ffn)
            load_tab(R_SH2, 0)
            sp.dma_start(x_res[1][:], xs[0]).then_inc(xr_in[1], 16)
            for j in (R_G1, R_A2, R_SH2):
                load_tab(j, 1)
            sp.wait_ge(merged_stored, 16 * 2 * KD)
            sp.dma_start(w_rt[:], w_router[0].rearrange("(k p) e -> p k e", p=P)).then_inc(router_in, 16)

            def load_m(t, b, src):
                sp.wait_ge(m_lo_done, t - 1)
                sp.dma_start(m_raw[b][:], merged_d[:, :, bass.ds(t * P, P)].rearrange("k p n -> p k n")).then_inc(m_in[b], 16)
                sp.wait_ge(x1_ready, t - 1)
                sp.dma_start(x_res[b][:], src).then_inc(xr_in[b], 16)

            def load_unit(e, j, first):
                w3 = (w_gate, w_up)[j % 2] if j < 8 else w_down
                q = j // 2 if j < 8 else j - 8
                if not first:
                    sp.wait_ge(unit_made, 12 * e - 12 + j + 1)
                sp.dma_start(wq[j][:], w3[0][bass.ds(e, 1), :, q * 2 * P:(q + 1) * 2 * P]
                             .rearrange("a (k p) n -> p (a k) n", p=P)).then_inc(wq_in[j], 16)

            sp.wait_ge(wo_lo_done, KD)
            for j in (8, 11):
                load_unit(0, j, True)
            with sp.Fori(0, 3) as i:
                for b in range(2):
                    load_m(2 * i + b + 2, b, xs[bass.ds(2 * i + b + 1, 1)].rearrange("a p d -> (a p) d"))
            load_m(8, 0, xs[7])

            sp.wait_ge(m_made, NT)
            load_unit(0, 0, True)
            load_unit(0, 1, True)
            sp.wait_ge(x1_sq, NT)
            sp.dma_start(flip[:], small_tab[:, N_SMALL:N_SMALL + P]).then_inc(flip_in, 16)
            for j in (*range(2, 8), 9, 10):
                load_unit(0, j, True)
            sp.wait_ge(h2_ready, NT)
            sp.wait_ge(h2_turned, NT)
            for b in range(2):
                sp.wait_ge(x1_stored[b], 16 * (5 - b))
                sp.wait_ge(h2_stored[b], 16 * (5 - b))
            for j in range(2):
                sp.dma_start(g2[:, j, :], mod_d[j:j + 1, R_G2 * D:(R_G2 + 1) * D].broadcast_to([P, D])).then_inc(g2_in, 16)
            sp.dma_start(norm_ffn[:], n_post_ffn[0:1, :].broadcast_to([P, D])).then_inc(norm_ffn_in, 16)

            with sp.Fori(1, EXPERTS) as e:
                for j in range(12):
                    load_unit(e, j, False)

            sp.wait_ge(unit_made, 12 * (EXPERTS - 1) + 5)
            sp.dma_start(x1_all[:], x1_d.rearrange("t p d -> p t d")).then_inc(x1_landed, 16)
            sp.wait_ge(added_l, 16 * EXPERTS)
            sp.wait_ge(added_c, 16 * EXPERTS)
            for g in range(3):
                sp.dma_start(f_all[:, 3 * g:3 * g + 3, :], ffn_d[3 * g * P:(3 * g + 3) * P, :].rearrange("(t p) d -> p t d", p=P))\
                  .then_inc(f_in_s[g], 16)
            for t in range(NT):
                sp.wait_ge(y_ready, t + 1)
                sp.dma_start(ys[t - 1] if t else yp, y_all[:, t, :]).then_inc(y_stored, 16)
            sp.wait_ge(y_stored, 16 * NT)

        @block.gpsimd
        def _(pool):
            pool.dma_start(lgt[:, 0, 0, :], dec_f[0:1, :].broadcast_to([P, HEADS])).then_inc(dec_in, 16)
            pool.dma_start(lgt[:, 0, 1, :], dec_b[0:1, :].broadcast_to([P, HEADS])).then_inc(dec_in, 16)
            pool.dma_start(lgt[0:DK, 0, 2, :], dec_f[0:1, :].broadcast_to([DK, HEADS])).then_inc(dec_in, 16)
            pool.dma_start(lgt[DK:P, 0, 2, :], dec_b[0:1, :].broadcast_to([DK, HEADS])).then_inc(dec_in, 16)

            pool_steps = Steps(pool, pool_step)

            def rstd(dst, src, eps):
                pool_steps.did(pool.tensor_tensor(dst, src, eps, ALU.add))
                pool_steps.settle()
                return pool.tensor_tensor(dst, dst, minus_half[:, 0:dst.shape[-1]], ALU.pow)

            pool.wait_ge(small_in, 16)

            pool.dma_start(s0[0:DK, :, :], state_f[0, 0].rearrange("h d e -> d h e")).then_inc(s0_in, 16)
            pool.dma_start(s0[DK:P, :, :], state_b[0, 0].rearrange("h d e -> d h e")).then_inc(s0_in, 16)
            pool.wait_ge(ss_done, NT)
            rstd(x_rstd, x_ms, rms_eps).then_inc(rstd_done, 1)

            with pool_steps.loop(HEADS, 3) as h:
                pool.wait_ge(state_ready, h + 1)
                plain(pool)
                pool.dma_start(new_f[0, 0, bass.ds(h, 1)].rearrange("a d e -> (a d) e"), state_out[0:DK, :]).then_inc(state_stored, 16)
                plain(pool)
                pool.dma_start(new_b[0, 0, bass.ds(h, 1)].rearrange("a d e -> (a d) e"), state_out[DK:P, :]).then_inc(state_stored, 16)
                for x in range(3):
                    pool.wait_ge(gn_var, 3 * h + x + 1)
                    ts = slice(CHUNKS[x][0], CHUNKS[x][-1] + 1)
                    rstd(gnr[:, ts], gnmv[:, ts, 1], gn_eps[:, 0:len(CHUNKS[x])]).then_inc(gn_rstd, 1)
            def store_share(n):
                pool.wait_ge(dve_evicted, ED_RETOUT + n + 1)
                pool.wait_ge(merged_stored, 16 * n)
                plain(pool)
                pool.dma_start(merged_d[bass.ds(n, 1)].rearrange("a p t -> (a p) t"), merged[:]).then_inc(merged_stored, 16)
                pool.wait_ge(mod_row_ready, n + 1)
                plain(pool)
                pool.dma_start(mod_d[:, bass.ds(512 * n, 512)].rearrange("(a w) n -> a w n", a=1), mod_row[:]).then_inc(mod_row_stored, 16)
            each(pool, KD, store_share)

            pool.wait_ge(projected, T_CONVOUT)
            for n in range(KD):
                pool.wait_ge(merged_ready, n)
                pool.wait_ge(conv_z, KD)
                pool.wait_ge(merged_stored, 16 * (KD + n))
                pool.dma_start(ret_part[:], merged_d[n]).then_inc(ret_part_in, 16)
                pool.wait_ge(merged_ready, n + 1)
                pool.dma_start(merged_d[n], merged[:]).then_inc(merged_stored, 16)

            def store(t, b):
                pool.wait_ge(m_sq, t + 1)
                rstd(stats[:, 8 + b:9 + b], stats[:, 4 + b:5 + b], rms_eps[:, 0:1]).then_inc(m_rstd, 1)
                pool.wait_ge(x1_ready, t + 1)
                plain(pool)
                pool.dma_start(x1_d[bass.ds(t, 1)].rearrange("a p d -> (a p) d"), x1[b][:]).then_inc(x1_stored[b], 16)
                pool.wait_ge(x1_sq, t + 1)
                rstd(stats[:, 12 + b:13 + b], stats[:, 6 + b:7 + b], rms_eps[:, 0:1]).then_inc(x1_rstd, 1)
                pool.wait_ge(h2_ready, t + 1)
                plain(pool)
                pool.dma_start(h2_d[bass.ds(t * P, P), :], h2[b][:]).then_inc(h2_stored[b], 16)

            with pool_steps.loop(4, 4) as i:
                store(2 * i, 0)
                store(2 * i + 1, 1)
            store(8, 0)
            pool.wait_ge(logit_made, NT)
            pool.memset(zero[:], 0.0).then_inc(zero_ready, 1)
            pool.wait_ge(zero_ready, 1)
            with pool.Fori(0, NT) as t:
                plain(pool)
                pool.dma_start(ffn_d[bass.ds(t * P, P), :], zero[:]).then_inc(ffn_zeroed, 16)
            pool.wait_ge(ffn_zeroed, 16 * NT)
            for b in range(2):
                pool.wait_ge(x1_stored[b], 16 * (5 - b))
                pool.wait_ge(h2_stored[b], 16 * (5 - b))

            def gather(e):
                if e:
                    pool.wait_ge(xg_turned, e)
                pool.indirect_dma_start(xg_l[:], None, h2_d, bass.IndirectOffsetOnAxis(ap=idx_l[:, e:e + 1], axis=0))\
                    .then_inc(got_l, 16)
                pool.indirect_dma_start(xg_c[:], None, h2_d, bass.IndirectOffsetOnAxis(ap=idx_c[:, e:e + 1], axis=0))\
                    .then_inc(got_c, 16)

            pool.wait_ge(sel_read, 4)
            gather(0)
            for e in range(EXPERTS):
                if e + 1 < EXPERTS:
                    gather(e + 1)
                pool.wait_ge(out_ready, 2 * e + 2)
                if e:
                    pool.wait_ge(added_l, 16 * e)
                    pool.wait_ge(added_c, 16 * e)
                pool.indirect_dma_start(ffn_d, bass.IndirectOffsetOnAxis(ap=idx_l[:, e:e + 1], axis=0), ot_l[:], None,
                                        compute_op=ALU.add).then_inc(added_l, 16)
                pool.indirect_dma_start(ffn_d, bass.IndirectOffsetOnAxis(ap=idx_c[:, e:e + 1], axis=0), ot_c[:], None,
                                        compute_op=ALU.add).then_inc(added_c, 16)

            pool.wait_ge(g2_ready, 2)
            for g in range(3):
                ts, t = slice(3 * g, 3 * g + 3), 3 * g + 2
                pool.wait_ge(f_in_s[g], 16)
                pool.tensor_tensor(y_all[:, t, :], f_all[:, t, :], g2[:, 1, :], ALU.mult).then_inc(f_scaled, 1)
                pool.wait_ge(f_sq, 3 * g + 3)
                rstd(f_rs[:, ts], f_ms[:, ts], rms_eps[:, ts]).then_inc(f_rstd, 1)
            pool.wait_ge(state_stored, 32 * HEADS)

        @block.tensor
        def _(pe):
            def bank(b, n):
                return ps[:, b, 0:n]

            pe.wait_ge(small_in, 16)
            pe.wait_ge(c_landed, 32)
            pe.transpose(bank(6, 2 * KD), c_in[:], ident[0:2 * KD, 0:2 * KD]).then_inc(c_turned, 1)

            def modulation(j):
                if j == 0:
                    pe.wait_ge(cond_ready, 1)
                pe.wait_ge(ada_in[j % 2], 16 * (j // 2 + 1))
                for k in range(KD):
                    mm = pe.matmul(ps[0:2, j, :], cond[:, k, :], ada[j % 2][:, k, :], start=(k == 0), stop=(k == KD - 1))
                mm.then_inc(ada_done, 1)

            def turn_x(t):
                pe.wait_ge(x_norm, t + 1)
                if t >= 2:
                    pe.wait_ge(x_feat, t - 1) if t < 8 else pe.wait_ge(x_feat_act, t - 7)
                for k in range(KD):
                    tr = pe.transpose(ps[:, 4 + 2 * (t % 2) + k // 4, (k % 4) * P:(k % 4 + 1) * P], xa[:, t, k * P:(k + 1) * P], ident)
                tr.then_inc(x_turned, 1)

            for j, tiles_after in enumerate(((), (0, 1), (2, 3, 4, 5), (6, 7))):
                modulation(j)
                for t in tiles_after:
                    turn_x(t)
            pe.wait_ge(vec_in_s, 16 * 4)
            pe.wait_ge(mrow_ready, 4)
            pe.transpose(bank(1, N_VEC), vec_in[:], ident[0:N_VEC, 0:N_VEC]).then_inc(vec_turned, 1)
            for j in range(2 * KD):
                tr = pe.transpose(ps[:, 0, 2 * j:2 * j + 2], mrow[:, j // 4, (j % 4) * P:(j % 4 + 1) * P], ident[0:2, 0:2])
            tr.then_inc(mod_turned, 1)
            turn_x(8)
            pe.wait_ge(mod_read, 1)

            def project(t, slot, hi, lo, blocks=range(NB), first=False):
                if 0 in blocks:
                    pe.wait_ge(w_lo_done, t + 1)
                for b in blocks:
                    for k in range(KD):
                        if first:
                            pe.wait_ge(h_lo_done, KD * b + k + 1)
                        out = ps[:, 3 * slot + b, 0:CB]
                        xh, xl = hi[:, k, b * CB:(b + 1) * CB], lo[:, k, b * CB:(b + 1) * CB]
                        pe.matmul(out, w_hi[:, slot, k, :], xh, start=(k == 0), stop=False)
                        pe.matmul(out, w_hi[:, slot, k, :], xl, start=False, stop=False)
                        mm = pe.matmul(out, w_lo[:, slot, k, :], xh, start=False, stop=(k == KD - 1))
                if NB - 1 in blocks:
                    mm.then_inc(projected, 1)

            def pair(i, first, last=False):
                def att(name, products):
                    for x in range(3):
                        if (name, x) not in ATT_AT:
                            continue
                        b = ATT_AT[name, x]
                        if b == 0:
                            pe.wait_ge(att_dve, N_ATT_BY["D"] * i - 3)
                            pe.wait_ge(att_act, N_ATT_BY["A"] * i)
                        elif not first or b >= 5:
                            if b >= 2:
                                n2, x2, who = ATT[b - 2]
                                pe.wait_ge(att_act if who == "A" else att_dve, att_reads(i, n2, x2))
                        mm = products(x, 6 + b % 2)
                        mm.then_inc(att_made, 1)

                def tile(t, blocks=range(NB)):
                    if first and t == 1:
                        pe.wait_ge(x_feat, 6)
                        pe.wait_ge(x_feat_act, 3)
                    if 0 in blocks and not (first and t < 2):
                        pe.wait_ge(act_evicted, 6 * i + t - 1) if t >= 2 else pe.wait_ge(act_evicted, 6 * i)
                    project(6 * i + t, t % 2, h_hi, h_lo, blocks, first=(first and t == 0))

                def halves(lhsT, src):
                    def products(x, b):
                        return pe.matmul(bank(b, 512), lhsT, src[:, 1 + 4 * x:5 + 4 * x, :], start=True, stop=True)
                    return products

                def turns(src):
                    def products(x, b):
                        for s, t in enumerate(CHUNKS[x]):
                            mm = pe.transpose(ps[:, b, s * P:(s + 1) * P], src[:, t, :], ident)
                        return mm
                    return products

                def scores(h):
                    def products(x, b):
                        r = slice(DK * h, DK * h + DK)
                        for s, t in enumerate(CHUNKS[x]):
                            mm = pe.matmul(ps[:, b, s * P:(s + 1) * P], kT[r, t, :], qT[r, t, :], start=True, stop=True)
                        return mm
                    return products

                def key_values(h):
                    def products(x, b):
                        for s, t in enumerate(CHUNKS[x]):
                            mm = pe.matmul(ps[:, b, s * P:(s + 1) * P], kz[h][:, t, :], v_tok[:, t, :], start=True, stop=True)
                        return mm
                    return products

                def outputs(x, b):
                    for s, t in enumerate(CHUNKS[x]):
                        o = ps[:, b, s * P:(s + 1) * P]
                        mm = pe.matmul(o, sm[:, t, :], v_tok[:, t, :], start=True, stop=(t == 0))
                        if t:
                            mm = pe.matmul(o, qx[:, t - 1, :], rs[:, t - 1, :], start=False, stop=True)
                    return mm

                if last:
                    att("before", turns(on))
                    return
                tile(0)
                if not first:
                    att("before", turns(on))
                tile(1)
                pe.wait_ge(act_evicted, 6 * i + 1)
                att("swap_q", halves(swap, qT))
                tile(2)
                pe.wait_ge(act_evicted, 6 * i + 2)
                att("swap_k", halves(swap, kT))
                tile(3, range(0, 1))
                pe.wait_ge(act_evicted, 6 * i + 3)
                att("v_tok0", turns(vT))
                tile(3, range(1, NB))
                pe.wait_ge(roped, 2 * i + 2)
                att("k_tok", turns(kT))
                tile(4, range(0, 1))
                att("dup0", halves(dup[0], qT))
                att("score0", scores(0))
                pe.wait_ge(att_act, att_reads(i, "k_tok", 2))
                att("kv0", key_values(0))
                tile(4, range(1, 2))
                pe.wait_ge(att_dve, att_reads(i, "kv0", 2))
                att("o0", outputs)
                tile(4, range(2, NB))
                tile(5, range(0, 1))
                pe.wait_ge(act_evicted, 6 * i + 4)
                att("v_tok1", turns(vT))
                att("dup1", halves(dup[1], qT))
                att("score1", scores(1))
                tile(5, range(1, 2))
                pe.wait_ge(att_dve, att_reads(i, "o0", 2))
                att("o_feat0", turns(on))
                pe.wait_ge(att_act, att_reads(i, "v_tok1", 2))
                att("kv1", key_values(1))
                tile(5, range(2, NB))
                pe.wait_ge(att_dve, att_reads(i, "kv1", 2))
                att("o1", outputs)

            pair(0, True)
            with pe.Fori(1, PAIRS) as i:
                pair(i, False)
            pair(PAIRS, False, last=True)

            def ret_out(n):
                pe.wait_ge(act_evicted, EA_RETOUT + n)
                project(T_RETOUT + 2 * n, 0, h_hi, h_lo)
                pe.wait_ge(z_lo_done, KD)
                pe.wait_ge(dve_evicted, ED_RETOUT + n)
                project(T_RETOUT + 2 * n + 1, 1, z_hi, z_lo)
                pe.wait_ge(ada_used, 8 * (n + 1))
                pe.wait_ge(mod_row_ready, n)
                for w_ in range(2):
                    mm = pe.matmul(ps[0:1, 6 + w_, :], mbwd[:, 0:1], ada_acc[:, w_, :], start=True, stop=True)
                mm.then_inc(ada_summed, 1)
            each(pe, KD, ret_out)

            with pe.Fori(0, KD // 2) as i:
                a, d, t = EA_CONV + 4 * i, ED_CONV + 2 * i, T_CONV + 6 * i
                for c_, (who, n) in enumerate(((act_evicted, a), (dve_evicted, d), (act_evicted, a + 1),
                                               (act_evicted, a + 2), (dve_evicted, d + 1), (act_evicted, a + 3))):
                    pe.wait_ge(who, n)
                    project(t + c_, c_ % 2, h_hi, h_lo)
            with pe.Fori(0, KD) as n:
                pe.wait_ge(act_evicted, EA_CONVOUT + n)
                project(T_CONVOUT + 2 * n, 0, h_hi, h_lo)
                pe.wait_ge(conv_z, KD)
                pe.wait_ge(dve_evicted, ED_CONVOUT + n)
                project(T_CONVOUT + 2 * n + 1, 1, z_hi, z_lo)

            def mix(n, b, half, first=False):
                if half == 0:
                    if first:
                        pe.wait_ge(m0_lo_most, 1)
                    else:
                        pe.wait_ge(m_lo_done, n + 1)
                        if not isinstance(n, int) or n > 1:
                            pe.wait_ge(x1_ready, n - 1)
                for k in range(KD):
                    if first:
                        pe.wait_ge(wo_lo_done, k + 1)
                        if k == KD - 1:
                            pe.wait_ge(m_lo_done, 1)
                    out = ps[:, 2 * b + half, :]
                    wh, wl = wo_hi[:, k, half * 512:half * 512 + 512], wo_lo[:, k, half * 512:half * 512 + 512]
                    pe.matmul(out, m_hi[b][:, k, :], wh, start=(k == 0), stop=False)
                    pe.matmul(out, m_hi[b][:, k, :], wl, start=False, stop=False)
                    mm = pe.matmul(out, m_lo[b][:, k, :], wh, start=False, stop=(k == KD - 1))
                if half:
                    mm.then_inc(m_made, 1)

            def turn_h2(n, b):
                pe.wait_ge(h2_ready, n + 1)
                pe.wait_ge(h2T_ready, n)
                for k in range(KD):
                    tr = pe.transpose(ps[:, 4 + k // 4, (k % 4) * P:(k % 4 + 1) * P], h2[b][:, k * P:(k + 1) * P], ident)
                tr.then_inc(h2_turned, 1)

            def route(n):
                pe.wait_ge(h2T_ready, n + 1)
                pe.wait_ge(logit_exp, n)
                for k in range(KD):
                    mm = pe.matmul(ps[:, 6, 0:EXPERTS], h2T[:, k, :], w_rt[:, k, :], start=(k == 0), stop=(k == KD - 1))
                mm.then_inc(logit_made, 1)

            pe.wait_ge(act_evicted, EA_CONVOUT + KD)
            mix(0, 0, 0, True)
            mix(0, 0, 1, True)
            pe.wait_ge(dve_evicted, ED_CONVOUT + KD)
            mix(1, 1, 0)
            mix(1, 1, 1)
            pe.wait_ge(router_in, 16)

            def mix_and_route(n, b):
                mix(n, b, 0)
                turn_h2(n - 2, b)
                mix(n, b, 1)
                route(n - 2)

            def two_tiles(i):
                mix_and_route(2 * i + 2, 0)
                mix_and_route(2 * i + 3, 1)
            each(pe, 3, two_tiles)

            mix_and_route(8, 0)
            for n in (7, 8):
                turn_h2(n, n % 2)
                route(n)
            pe.wait_ge(aff_done, NT)
            for t in range(HALF_T):
                pe.transpose(ps[0:E2 + EXPERTS, 0, t * P:(t + 1) * P], aff[:, 1 + t, :, :].rearrange("p a e -> p (a e)"), ident)
            pe.transpose(ps[0:EXPERTS, 1, 0:P], aff[:, 0, 0, :], ident).then_inc(aff_turned, 1)
            pe.wait_ge(sel_ready, 2)
            id16, id48 = ident[0:EXPERTS, 0:EXPERTS], ident[0:E2 + EXPERTS, 0:E2 + EXPERTS]
            pe.transpose(ps[:, 4, 0:48], sel_v[:, 0:CAP_L], id48)
            pe.transpose(ps[:, 4, 48:96], sel_f[:, 0:CAP_L], id48)
            pe.transpose(ps[0:CAP_C, 4, 96:112], sel_v[0:EXPERTS, CAP_L:CAP], id16)
            pe.transpose(ps[0:CAP_C, 4, 112:128], sel_f[0:EXPERTS, CAP_L:CAP], id16).then_inc(sel_turned, 1)
            pe.wait_ge(flip_in, 16)
            pe.wait_ge(sel_copied, 1)
            pe.matmul(ps[:, 5, 0:2 * EXPERTS], flip[:], halves[:, :, E2:E2 + EXPERTS], start=True, stop=True).then_inc(sel_flipped, 1)

            def turn_rows(e):
                pe.wait_ge(got_l, 16 * (e + 1))
                pe.wait_ge(got_c, 16 * (e + 1))
                for k in range(KD):
                    pe.transpose(ps[:, 4 + k // 4, (k % 4) * P:(k % 4 + 1) * P], xg_l[:, k * P:(k + 1) * P], ident)
                for k in range(KD):
                    tr = pe.transpose(ps[:, 6, k * CAP_C:(k + 1) * CAP_C], xg_c[:, k * P:(k + 1) * P], id16)
                tr.then_inc(xg_turned, 1)

            def unit(e, j, src):
                pe.wait_ge(wq_in[j], 16 * (e + 1))
                for m in range(2):
                    for k in range(KD):
                        mm = pe.matmul(ps[:, j % 4, m * CAP:(m + 1) * CAP], wq[j][:, k, m * P:(m + 1) * P], src[:, k, :],
                                       start=(k == 0), stop=(k == KD - 1))
                mm.then_inc(unit_made, 1)

            def expert(e, last):
                pe.wait_ge(xT_ready, 2 * e + 2)
                for j in range(8):
                    if j < 4:
                        pe.wait_ge(unit_act, 8 * e)
                    elif j % 2:
                        pe.wait_ge(unit_dve, 4 * e + (j - 3) // 2)
                    else:
                        pe.wait_ge(unit_act, 8 * e + (j - 2) // 2)
                    unit(e, j, xT)
                if not last:
                    pe.wait_ge(out_ready, 2 * e)
                    turn_rows(e + 1)
                pe.wait_ge(unit_act, 8 * e + 4)
                pe.wait_ge(unit_dve, 4 * e + 4)
                for j in range(8, 12):
                    unit(e, j, hid)
                pe.wait_ge(unit_act, 8 * e + 8)
                if not last:
                    pe.wait_ge(xT_ready, 2 * e + 4)
                else:
                    pe.wait_ge(out_ready, 2 * e)
                for k in range(KD):
                    pe.transpose(ps[:, 4 + k // 4, (k % 4) * P:(k % 4 + 1) * P], outT[:, k, 0:CAP_L], ident)
                for k in range(KD):
                    tr = pe.transpose(ps[0:CAP_C, 6 + k // 4, (k % 4) * P:(k % 4 + 1) * P], outT[:, k, CAP_L:CAP], ident)
                tr.then_inc(out_turned, 1)

            pe.wait_ge(affT_ready, 1)
            pe.wait_ge(sel_read, 4)
            turn_rows(0)
            expert(0, False)
            with pe.Fori(1, EXPERTS - 1) as e:
                expert(e, False)
            expert(EXPERTS - 1, True)

        @block.scalar
        def _(act):
            steps = Steps(act, act_step)
            did, settle = steps.did, steps.settle

            for row, v in ((V_BADA, b_ada[0, 0:2 * D]), (V_PREMIX, n_pre_mix[0]), (V_GN, gn_g[0]),
                           (V_CONV, conv_w[0].rearrange("t d -> (t d)"))):
                n = v.shape[0] // P
                act.dma_start(vec_in[row:row + n, :], v.rearrange("(r p) -> r p", p=P)).then_inc(vec_in_s, 16)
            act.wait_ge(c_turned, 1)
            act.activation(cond[:], ps[:, 6, 0:2 * KD].rearrange("p (w k) -> p k w", w=2), ACT.Silu).then_inc(cond_ready, 1)

            act.wait_ge(lg_part, 1)
            act.activation(lgt[:, 1], lgt[:, 1], ACT.Exp).then_inc(lg_exp, 1)

            act.wait_ge(x_landed, 32)
            def square_x(t):
                act.wait_ge(ss_done, t)
                plain(act)
                act.activation(sq[:], xa[:, bass.ds(t, 1), :].rearrange("p a n -> p (a n)"), ACT.Square, scale=D ** -0.5,
                               accum_out=x_ms[:, bass.ds(t, 1)]).then_inc(ss_done, 1)
            each(act, NT, square_x)

            act.wait_ge(rstd_done, 1)
            with act.Fori(0, NT) as t:
                at_ = bass.ds(t, 1)
                act.activation(xa[:, at_, :], xa[:, at_, :], ACT.Copy, scale=x_rstd[:, at_]).then_inc(x_norm, 1)

            act.wait_ge(lg_ready, 1)
            for h in range(HEADS):
                did(act.activation(decay[:, h, :], fwd, ACT.Exp, scale=lg[:, 0, h:h + 1]))
                did(act.activation(e2[:, h, :], bwd, ACT.Exp, scale=lg[:, 1, h:h + 1]))
                did(act.activation(xi[:, h, :], xarg, ACT.Exp, scale=lg[:, 2, h:h + 1]))
            did(act.activation(zeta[:, 0, :], lg[:, 0, :], ACT.Exp, scale=pos[:, 0:1]))
            did(act.activation(zeta[:, 1, :], lg[:, 1, :], ACT.Exp, scale=pos[:, 1:2]))
            act.activation(gchunk[:], lg[:, 2, :], ACT.Exp, scale=pos[:, 2:3]).then_inc(exp_ready, 1)

            def split(t0, per, i, c_):
                act.wait_ge(w_in_s[c_ % 2], 16 * ((t0 + c_) // 2 + 1) + 16 * (per // 2) * i)
                if t0 + c_ >= 2:
                    act.wait_ge(projected, t0 + c_ - 1 + per * i)
                act.copy(w_hi[:, c_ % 2], w_raw[:, c_ % 2]).then_inc(w_hi_done, 1)

            def out_of(slot):
                return ps[:, 3 * slot:3 * slot + NB, 0:CB]

            def evict(t, slot, dst, func, scale=1.0):
                act.wait_ge(projected, t + 1)
                plain(act)
                act.activation(dst.rearrange("p (b n) -> p b n", b=NB), out_of(slot), func, scale=scale)\
                   .then_inc(act_evicted, 1)

            def flat(t):
                return t[:].rearrange("p t n -> p (t n)")

            split(0, 6, 0, 0)
            def features(t):
                act.wait_ge(x_turned, t + 1)
                b = 4 + 2 * (t % 2)
                act.copy(xF[:, :, t * P:(t + 1) * P], ps[:, b:b + 2, :].rearrange("p a (k n) -> p (a k) n", n=P))\
                   .then_inc(x_feat_act, 1)

            features(6)
            features(7)
            act.wait_ge(scale_ready, 1)
            for b in range(NB):
                if b < 2:
                    act.wait_ge(x_feat, 3 * b + 3)
                else:
                    act.wait_ge(x_feat_act, 3)
                with act.Fori(0, KD) as k:
                    for w_, at_ in parts_of(b):
                        ins = act.activation(h_hi[:, bass.ds(k, 1), at_], xF[:, bass.ds(k, 1), at_], ACT.Identity,
                                             bias=modT[:, bass.ds(k, 1), w_], scale=scale1[:, bass.ds(k, 1), w_])
                    ins.then_inc(h_hi_done, 1)
                if b == 0:
                    features(8)
            act.wait_ge(exp_ready, 1)
            def pair(i):
                def att(name, read):
                    for x in range(3):
                        b = ATT_AT[name, x]
                        act.wait_ge(att_made, att_count(i, name, x))
                        plain(act)
                        read(x, ps[:, 6 + b % 2, 0:P * len(CHUNKS[x])].rearrange("p (t n) -> p t n", n=P)).then_inc(att_act, 1)

                def key_weights(x, src):
                    ts = slice(CHUNKS[x][0], CHUNKS[x][-1] + 1)
                    for h in range(2):
                        for d in range(2):
                            ins = act.activation(kz[h][:, ts, d * DK:(d + 1) * DK], src[:, :, h * DK:(h + 1) * DK], ACT.Copy,
                                                 scale=zeta2[:, d, h:h + 1])
                            if h + d < 2:
                                did(ins)
                    return ins

                def values(x, src):
                    return act.copy(v_tok[:, CHUNKS[x][0]:CHUNKS[x][-1] + 1, :], src)

                def z_of(h):
                    return z_ret[:, bass.ds(2 * i + h, 1), :].rearrange("p a t -> p (a t)")

                did(act.copy(zeta2[:], zeta[:, :, bass.ds(2 * i, 2)]))
                settle()
                split(0, 6, i, 1)
                evict(6 * i, 0, flat(qT), ACT.Copy)
                split(0, 6, i, 2)
                evict(6 * i + 1, 1, flat(kT), ACT.Copy, scale=DK ** -0.5)
                split(0, 6, i, 3)
                evict(6 * i + 2, 0, flat(vT), ACT.Copy)
                att("v_tok0", values)
                split(0, 6, i, 4)
                evict(6 * i + 3, 1, flat(vT), ACT.Copy)
                att("k_tok", key_weights)
                split(0, 6, i, 5)
                evict(6 * i + 4, 0, z_of(0), ACT.Silu)
                att("v_tok1", values)
                split(0, 6, i, 6)
                evict(6 * i + 5, 1, z_of(1), ACT.Silu)

            pair(0)
            with steps.loop(PAIRS, 10, start=1) as i:
                pair(i)

            act.wait_ge(att_dve, READS_D)
            for k in range(KD):
                act.copy(z_hi[:, k, :], z_ret[:, k, :]).then_inc(z_hi_done, 1)
            def ret_gate(n):
                split(T_RETOUT, 2, n, 1)
                act.wait_ge(dve_evicted, ED_RETOUT + n)
                evict(T_RETOUT + 2 * n, 0, gate[:], ACT.Sigmoid)
                split(T_RETOUT, 2, n, 2)
            each(act, KD, ret_gate)

            def conv_tiles(i):
                for s in range(2):
                    j = 2 * i + s
                    split(T_CONV, 6, i, 3 * s + 1)
                    act.wait_ge(conv_z, j)
                    if s == 0:
                        act.wait_ge(merged_stored, 16 * KD)
                    evict(T_CONV + 3 * j, s, cbT[:], ACT.Copy)
                    split(T_CONV, 6, i, 3 * s + 2)
                    evict(T_CONV + 3 * j + 1, 1 - s, ccT[:], ACT.Copy)
                    split(T_CONV, 6, i, 3 * s + 3)
                    act.wait_ge(conv_z_raw, j + 1)
                    plain(act)
                    act.copy(z_hi[:, bass.ds(j, 1), :].rearrange("p a t -> p (a t)"), ccT[:]).then_inc(z_hi_done, 1)
            each(act, KD // 2, conv_tiles)


            def gate_out(n, last):
                split(T_CONVOUT, 2, n, 1)
                act.wait_ge(dve_evicted, ED_CONVOUT + n)
                act.wait_ge(conv_z, KD)
                evict(T_CONVOUT + 2 * n, 0, gate[:], ACT.Sigmoid)
                if not last:
                    split(T_CONVOUT, 2, n, 2)

            with act.Fori(0, KD - 1) as n:
                gate_out(n, False)
            gate_out(KD - 1, True)

            def high_wo(k):
                act.wait_ge(wo_in[k % 4], 16 * (k // 4 + 1))
                act.copy(wo_hi[:, k, :], wo_raw[k % 4].rearrange("p k n -> p (k n)")).then_inc(wo_hi_done, 1)

            def high_of_first(b):
                act.wait_ge(m_in[b], 16)
                ins = act.copy(m_hi[b][:, 0:KD - 1, :], m_raw[b][:, 0:KD - 1, :])
                if b == 0:
                    ins.then_inc(m0_hi_most, 1)

            def high_of_last(b):
                act.wait_ge(merged_ready, KD)
                act.copy(m_hi[b][:, KD - 1, :], merged[:, b * P:(b + 1) * P]).then_inc(m_hi_done, 1)

            act.wait_ge(projected, T_WO - 1)
            high_wo(0)
            high_of_first(0)
            for k in range(1, 6):
                high_wo(k)
            high_of_last(0)
            high_wo(6)
            high_wo(7)
            act.wait_ge(projected, T_WO)
            high_of_first(1)
            high_of_last(1)

            def high_m(n, b, landed):
                act.wait_ge(m_in[b], landed)
                act.wait_ge(m_made, n - 1)
                act.copy(m_hi[b][:], m_raw[b][:]).then_inc(m_hi_done, 1)

            def square_m(n, b):
                act.wait_ge(m_made, n + 1)
                act.wait_ge(x1_sq, n)
                act.activation(sq2[:].rearrange("p (a n) -> p a n", a=2), ps[:, 2 * b:2 * b + 2, :], ACT.Square, scale=D ** -0.5,
                               accum_out=stats[:, 4 + b:5 + b]).then_inc(m_sq, 1)

            def square_x1(n, b):
                act.wait_ge(x1_ready, n + 1)
                act.wait_ge(m_sq, n + 1)
                act.activation(sq2[:], x1[b][:], ACT.Square, scale=D ** -0.5, accum_out=stats[:, 6 + b:7 + b]).then_inc(x1_sq, 1)

            def h2_features(n):
                act.wait_ge(h2_turned, n + 1)
                if not isinstance(n, int) or n:
                    act.wait_ge(logit_made, n)
                act.copy(h2T[:].rearrange("p (a k) n -> p a (k n)", a=2), ps[:, 4:6, :]).then_inc(h2T_ready, 1)

            def exp_logits(n):
                act.wait_ge(logit_max, n + 1)
                plain(act)
                act.activation(aff_of(n), ps[:, 6, 0:EXPERTS], ACT.Exp,
                               bias=stats[:, 10:11], accum_out=stats[:, 11:12]).then_inc(logit_exp, 1)

            def mix_step(n, b, landed=None, square=True):
                if square:
                    square_m(n - 1, 1 - b)
                if not isinstance(n, int) or n >= 3:
                    exp_logits(n - 3)
                if landed is not None:
                    high_m(n + 1, 1 - b, landed)
                if square:
                    square_x1(n - 1, 1 - b)
                if not isinstance(n, int) or 2 <= n <= 10:
                    h2_features(n - 2)

            act.wait_ge(m_lo_done, 2)
            act.wait_ge(merged_stored, 16 * 2 * KD)
            mix_step(1, 1, 32)
            mix_step(2, 0, 32)
            with act.Fori(0, 2) as i:
                mix_step(2 * i + 3, 1, 16 * (i + 3))
                mix_step(2 * i + 4, 0, 16 * (i + 3))
            mix_step(7, 1, 16 * 5)
            mix_step(8, 0)
            mix_step(9, 1)
            mix_step(10, 0, square=False)
            mix_step(11, 1, square=False)

            def rows_to_xT(e):
                act.wait_ge(xg_turned, e + 1)
                act.copy(xT[:, :, 0:CAP_L], ps[:, 4:6, :].rearrange("p a (k n) -> p (a k) n", n=P)).then_inc(xT_ready, 1)
                act.copy(xT[:, :, CAP_L:CAP], ps[:, 6, 0:KD * CAP_C].rearrange("p (k n) -> p k n", n=CAP_C)).then_inc(xT_ready, 1)

            def unit_of(j):
                return ps[:, j % 4, 0:2 * CAP].rearrange("p (m n) -> p m n", m=2)

            def expert(e, last):
                for q in range(4):
                    act.wait_ge(unit_made, 12 * e + 2 * q + 1)
                    act.wait_ge(unit_dve, 4 * e + q)
                    act.activation(sg[:], unit_of(2 * q), ACT.Silu).then_inc(unit_act, 1)
                if not last:
                    rows_to_xT(e + 1)
                act.wait_ge(out_turned, e)
                for q in range(4):
                    act.wait_ge(unit_made, 12 * e + 9 + q)
                    act.copy(outT[:, 2 * q:2 * q + 2, :], unit_of(8 + q)).then_inc(unit_act, 1)

            rows_to_xT(0)
            expert(0, False)
            with act.Fori(1, EXPERTS - 1) as e:
                expert(e, False)
            expert(EXPERTS - 1, True)

            for t in range(NT):
                act.wait_ge(f_in_s[t // 3], 16)
                if t:
                    act.wait_ge(f_sq, t)
                act.activation(sq3[:], f_all[:, t, :], ACT.Square, scale=D ** -0.5, accum_out=f_ms[:, t:t + 1]).then_inc(f_sq, 1)

        @block.vector
        def _(dve):
            steps = Steps(dve, dve_step)
            did, settle = steps.did, steps.settle

            def over(t, n):
                return t.unsqueeze(1).broadcast_to([P, n, t.shape[-1]])

            def along(t, n):
                return t.unsqueeze(2).broadcast_to([P, t.shape[1], n])

            dve.wait_ge(dec_in, 64)
            dve.scalar_tensor_tensor(lgt[:, 1], lgt[:, 0], -1.0, lgt[:, 0], ALU.mult, ALU.min).then_inc(lg_part, 1)
            did(dve.tensor_scalar(lg[:], lgt[:, 0], 0.0, None, ALU.min))
            dve.wait_ge(lg_exp, 1)
            e_, s_, s2, acc = lgt[:, 1], lgt[:, 2], lgt[:, 3], lgt[:, 4]
            did(dve.tensor_scalar(s_, e_, 2.0, None, ALU.add))
            settle()
            did(dve.reciprocal(s_, s_))
            settle()
            did(dve.tensor_tensor(s_, s_, e_, ALU.mult))
            settle()
            did(dve.tensor_tensor(s2, s_, s_, ALU.mult))
            settle()
            did(dve.tensor_scalar(acc, s2, 1.0 / 19, None, ALU.mult))
            for n in (17, 15, 13, 11, 9, 7, 5, 3):
                settle()
                did(dve.scalar_tensor_tensor(acc, acc, 1.0 / n, s2, ALU.add, ALU.mult))
            settle()
            did(dve.scalar_tensor_tensor(acc, acc, 1.0, s_, ALU.add, ALU.mult))
            settle()
            dve.scalar_tensor_tensor(lg[:], acc, -2.0, lg[:], ALU.mult, ALU.add).then_inc(lg_ready, 1)

            def row_out(j):
                dve.wait_ge(ada_done, j + 1)
                dve.tensor_copy(mrow[:, j, :], ps[0:2, j, :]).then_inc(mrow_ready, 1)

            def features(t):
                dve.wait_ge(x_turned, t + 1)
                b = 4 + 2 * (t % 2)
                dve.tensor_copy(xF[:, :, t * P:(t + 1) * P], ps[:, b:b + 2, :].rearrange("p a (k n) -> p (a k) n", n=P))\
                   .then_inc(x_feat, 1)

            def low_h(b):
                dve.wait_ge(x_feat, 3 * b + 3) if b < 2 else dve.wait_ge(x_feat_act, 3)
                with steps.loop(KD // 2, 2 * len(parts_of(b))) as k2:
                    for k in range(2):
                        at_k = bass.ds(2 * k2 + k, 1)
                        dve.wait_ge(h_hi_done, KD * b + 2 * k2 + k + 1)
                        for w_, at_ in parts_of(b):
                            did(dve.tensor_scalar(xF[:, at_k, at_], xF[:, at_k, at_], scale1[:, at_k, w_], modT[:, at_k, w_],
                                                  ALU.mult, ALU.add))
                    for k in range(2):
                        if k == 0 and b:
                            steps.settle_but_last()
                        else:
                            settle()
                        at_k, at_ = bass.ds(2 * k2 + k, 1), slice(b * CB, (b + 1) * CB)
                        dve.tensor_tensor(h_lo[:, at_k, at_], xF[:, at_k, at_], h_hi[:, at_k, at_].bitcast(F32), ALU.subtract)\
                           .then_inc(h_lo_done, 1)

            def split(t0, per, i, c_):
                dve.wait_ge(w_hi_done, t0 + per * i + c_ + 1)
                dve.tensor_tensor(w_lo[:, c_ % 2], w_raw[:, c_ % 2], w_hi[:, c_ % 2].bitcast(F32), ALU.subtract)\
                   .then_inc(w_lo_done, 1)

            row_out(0)
            for j, tiles_after in ((1, (0, 1)), (2, (2, 3, 4, 5))):
                row_out(j)
                for t in tiles_after:
                    features(t)

            dve.wait_ge(exp_ready, 1)
            did(dve.tensor_tensor(decay[:], decay[:], over(mfwd, HEADS), ALU.mult))
            did(dve.tensor_tensor(e2[:], e2[:], over(mbwd, HEADS), ALU.mult))
            settle()
            did(dve.tensor_tensor(decay[:], decay[:], e2[:], ALU.add))
            settle()

            split(0, 6, 0, 0)
            row_out(3)
            dve.wait_ge(vec_turned, 1)
            dve.tensor_copy(vecT[:], ps[:, 1, 0:N_VEC]).then_inc(vec_ready, 1)
            dve.wait_ge(vec_ready, 1)
            dve.wait_ge(mod_turned, 1)
            dve.tensor_tensor(modT[:], ps[:, 0, 0:4 * KD].rearrange("p (k w) -> p k w", w=2), along(vecT[:, V_BADA:V_BADA + 2 * KD], 2),
                              ALU.add).then_inc(mod_read, 1)
            dve.wait_ge(mod_read, 1)
            dve.scalar_tensor_tensor(scale1[:], modT[:, KD:2 * KD, :], 1.0,
                                     along(vecT[:, V_PREMIX:V_PREMIX + KD], 2), ALU.add, ALU.mult).then_inc(scale_ready, 1)
            dve.wait_ge(scale_ready, 1)
            low_h(0)
            low_h(1)
            low_h(2)

            def tiles(t):
                return t.rearrange("p (t n) -> p t n", n=P)

            dve.wait_ge(rope_in, 16)
            dve.wait_ge(s0_in, 32)
            def pair(i, first, last=False):
                def made(name, x):
                    dve.wait_ge(att_made, att_count(i, name, x))

                def own(name, x):
                    dve.wait_ge(att_dve, att_reads(i, name, x))

                def read(name, x, n=None):
                    b = 6 + ATT_AT[name, x] % 2
                    return ps[:, b, 0:(n or P * len(CHUNKS[x]))].rearrange("p (t n) -> p t n", n=P)

                def span(x):
                    return slice(CHUNKS[x][0], CHUNKS[x][-1] + 1)

                def rotate(name, dst, nth):
                    for x in range(2):
                        made(name, x)
                        dve.tensor_tensor(tiles(tmp[:, 512 * x:512 * x + 512]), read(name, x, 512),
                                          tiles(rope[:, 1, 512 * x:512 * x + 512]), ALU.mult).then_inc(att_dve, 1)
                    did(dve.tensor_tensor(dst[:, 1:NT, :], dst[:, 1:NT, :], tiles(rope[:, 0, :]), ALU.mult))
                    settle()
                    own(name, 1)
                    dve.tensor_tensor(dst[:, 1:NT, :], dst[:, 1:NT, :], tiles(tmp[:]), ALU.add).then_inc(roped, 1)
                    dve.wait_ge(roped, 2 * i + nth)

                def duplicate(h):
                    for x in range(2):
                        made(f"dup{h}", x)
                        dve.tensor_tensor(qx[:, 4 * x:4 * x + 4, :], read(f"dup{h}", x, 512),
                                          xi[:, bass.ds(2 * i + h, 1), :].broadcast_to([P, 4, P]), ALU.mult).then_inc(att_dve, 1)

                def scores(h):
                    for x in range(3):
                        made(f"score{h}", x)
                        dve.tensor_tensor(sm[:, span(x), :], read(f"score{h}", x),
                                          decay[:, bass.ds(2 * i + h, 1), :].broadcast_to([P, len(CHUNKS[x]), P]),
                                          ALU.mult).then_inc(att_dve, 1)

                def states(h):
                    head = 2 * i + h
                    made(f"kv{h}", 0)
                    dve.wait_ge(state_stored, 32 * head)
                    dve.tensor_copy(state_out[:], ps[:, 6 + ATT_AT[f"kv{h}", 0] % 2, 0:P]).then_inc(state_ready, 1)
                    did(dve.tensor_copy(rs[DK:P, 7, :], s0[DK:P, bass.ds(head, 1), :].rearrange("p a e -> p (a e)")))
                    dve.tensor_copy(rs[0:DK, 0, :], s0[0:DK, bass.ds(head, 1), :].rearrange("p a e -> p (a e)")).then_inc(att_dve, 1)
                    made(f"kv{h}", 2)
                    own(f"kv{h}", 0)

                    def update(part, src, dst):
                        b = 6 + ATT_AT[f"kv{h}", 1 + src // 4] % 2
                        return dve.scalar_tensor_tensor(rs[part, dst, :], rs[part, src, :], gchunk[part, bass.ds(head, 1)],
                                                        ps[part, b, (src % 4) * P:(src % 4 + 1) * P], ALU.mult, ALU.add)
                    for s in range(6):
                        settle()
                        did(update(slice(0, DK), s, s + 1))
                        did(update(slice(DK, P), 7 - s, 6 - s))
                    settle()
                    update(slice(DK, P), 1, 0).then_inc(att_dve, 1)
                    update(slice(0, DK), 6, 7).then_inc(att_dve, 1)

                def normalise(h):
                    for x in range(3):
                        made(f"o{h}", x)
                        src = read(f"o{h}", x)
                        for s, t in enumerate(CHUNKS[x]):
                            did(dve.bn_stats(gn6[:, t, :], src[:, s, :]))
                        settle()
                        did(dve.memset(stats[:, 30:31], 0.0))
                        for t in CHUNKS[x]:
                            ins = dve.bn_aggr(gnmv[:, t, :], gn6[:, t, :])
                            if t == CHUNKS[x][-1]:
                                ins.then_inc(gn_var, 1)
                            else:
                                did(ins)
                        dve.wait_ge(gn_rstd, 6 * i + 3 * h + x + 1)
                        for s, t in enumerate(CHUNKS[x]):
                            ins = dve.tensor_scalar(on[:, t, :], src[:, s, :], gnmv[:, t, 0:1], gnr[:, t:t + 1],
                                                    ALU.subtract, ALU.mult)
                            if t == CHUNKS[x][-1]:
                                ins.then_inc(att_dve, 1)
                            else:
                                did(ins)

                def gated(name, head, evicted):
                    dve.wait_ge(act_evicted, evicted)
                    for x in range(3):
                        made(name, x)
                        z = z_ret[:, bass.ds(head, 1), P * CHUNKS[x][0]:P * CHUNKS[x][-1] + P].rearrange("p a t -> p (a t)")
                        dve.scalar_tensor_tensor(z, ps[:, 6 + ATT_AT[name, x] % 2, 0:P * len(CHUNKS[x])],
                                                 vecT[:, bass.ds(V_GN + head, 1)], z, ALU.mult, ALU.mult).then_inc(att_dve, 1)

                if last:
                    gated("before", 2 * i - 1, 6 * i)
                    return
                split(0, 6, i, 1)
                if not first:
                    gated("before", 2 * i - 1, 6 * i)
                split(0, 6, i, 2)
                rotate("swap_q", qT, 1)
                split(0, 6, i, 3)
                rotate("swap_k", kT, 2)
                split(0, 6, i, 4)
                duplicate(0)
                scores(0)
                split(0, 6, i, 5)
                states(0)
                normalise(0)
                duplicate(1)
                scores(1)
                gated("o_feat0", 2 * i, 6 * i + 5)
                states(1)
                split(0, 6, i, 6)
                normalise(1)

            pair(0, True)
            with steps.loop(PAIRS, 76, start=1) as i:
                pair(i, False)
            pair(PAIRS, False, last=True)

            for k in range(KD):
                dve.wait_ge(z_hi_done, k + 1)
                dve.tensor_tensor(z_lo[:, k, :], z_ret[:, k, :], z_hi[:, k, :].bitcast(F32), ALU.subtract).then_inc(z_lo_done, 1)

            def banks(t):
                return t[:].rearrange("p (b n) -> p b n", b=NB)

            def ret_merge(n):
                split(T_RETOUT, 2, n, 1)
                dve.wait_ge(ada_summed, n)
                for k in range(KD):
                    dve.wait_ge(ada_k_in[k % 2], 64 * n + 16 * (k // 2) + 16)
                    if k:
                        settle()
                        dve.wait_ge(ada_used, 8 * n + k)
                    for w_ in range(2):
                        if k == 0:
                            ins = dve.tensor_scalar(ada_acc[:, w_, :], ada_k[0][:], cond[:, 0, w_:w_ + 1], None, ALU.mult)
                        else:
                            ins = dve.scalar_tensor_tensor(ada_acc[:, w_, :], ada_k[k % 2][:], cond[:, k, w_:w_ + 1],
                                                           ada_acc[:, w_, :], ALU.mult, ALU.add)
                        if w_:
                            ins.then_inc(ada_used, 1)
                        else:
                            did(ins)
                split(T_RETOUT, 2, n, 2)
                dve.wait_ge(projected, T_RETOUT + 2 * n + 2)
                dve.wait_ge(act_evicted, EA_RETOUT + n + 1)
                dve.wait_ge(merged_stored, 16 * n)
                dve.tensor_tensor(banks(merged), ps[:, 3:6, 0:CB], banks(gate), ALU.mult).then_inc(dve_evicted, 1)
                dve.wait_ge(ada_summed, n + 1)
                dve.wait_ge(b_row_in, 16 * (n + 1))
                dve.wait_ge(mod_row_stored, 16 * n)
                did(dve.tensor_tensor(mod_row[:, 0, :], ps[0:1, 6, :], b_row[:], ALU.add))
                dve.tensor_tensor(mod_row[:, 1, :], ps[0:1, 7, :], b_row[:], ALU.add).then_inc(mod_row_ready, 1)
            steps.each(KD, 9, ret_merge)


            dve.wait_ge(ada_used, 8 * KD)
            dve.wait_ge(mod_row_ready, KD)
            dve.wait_ge(mod_row_stored, 16 * KD)
            settle()
            for x in (0, CTX + 1, TOK + 2):
                did(dve.memset(prod[:, x:x + 1], 0.0))
            with steps.loop(KD // 2, 12) as i:
                for s in range(2):
                    j = 2 * i + s
                    for c_ in range(3):
                        split(T_CONV, 6, i, 3 * s + c_ + 1)
                    dve.wait_ge(projected, T_CONV + 3 * j + 3)
                    dve.wait_ge(act_evicted, EA_CONV + 2 * j + 2)
                    b0 = 3 * s
                    did(dve.tensor_tensor(prod[:, 1:1 + CTX], ps[:, b0, 0:CTX], ccT[:, 0:CTX], ALU.mult))
                    did(dve.tensor_tensor(prod[:, CTX + 2:CB + 2], ps[:, b0, CTX:CB], ccT[:, CTX:CB], ALU.mult))
                    dve.tensor_tensor(prod[:, CB + 2:TOK + 2].rearrange("p (b n) -> p b n", n=CB), ps[:, b0 + 1:b0 + 3, 0:CB],
                                      ccT[:, CB:TOK].rearrange("p (b n) -> p b n", n=CB), ALU.mult).then_inc(dve_evicted, 1)
                    dve.wait_ge(dve_evicted, ED_CONV + j + 1)
                    settle()
                    did(dve.tensor_scalar(u[:, 0:TOK + 1], prod[:, 0:TOK + 1], vecT[:, bass.ds(V_CONV + j, 1)], None, ALU.mult))
                    for tap in (1, 2):
                        settle()
                        did(dve.scalar_tensor_tensor(u[:, 0:TOK + 1], prod[:, tap:TOK + 1 + tap],
                                                     vecT[:, bass.ds(V_CONV + KD * tap + j, 1)], u[:, 0:TOK + 1], ALU.mult, ALU.add))
                    settle()
                    did(dve.tensor_tensor(ccT[:, 0:CTX], cbT[:, 0:CTX], u[:, 0:CTX], ALU.mult))
                    dve.tensor_tensor(ccT[:, CTX:TOK], cbT[:, CTX:TOK], u[:, CTX + 1:TOK + 1], ALU.mult).then_inc(conv_z_raw, 1)
                    dve.wait_ge(conv_z_raw, j + 1)
                    dve.wait_ge(z_hi_done, KD + j + 1)
                    dve.tensor_tensor(z_lo[:, bass.ds(j, 1), :].rearrange("p a t -> p (a t)"), ccT[:],
                                      z_hi[:, bass.ds(j, 1), :].rearrange("p a t -> p (a t)").bitcast(F32), ALU.subtract)\
                       .then_inc(conv_z, 1)

            def merge(n):
                dve.wait_ge(projected, T_CONVOUT + 2 * n + 2)
                dve.wait_ge(act_evicted, EA_CONVOUT + n + 1)
                dve.wait_ge(merged_stored, 16 * (KD + n))
                dve.tensor_tensor(banks(merged), ps[:, 3:6, 0:CB], banks(gate), ALU.mult).then_inc(dve_evicted, 1)
                dve.wait_ge(dve_evicted, ED_CONVOUT + n + 1)
                dve.wait_ge(ret_part_in, 16 * (n + 1))
                dve.tensor_tensor(merged[:], merged[:], ret_part[:], ALU.add).then_inc(merged_ready, 1)

            with dve.Fori(0, KD - 1) as n:
                split(T_CONVOUT, 2, n, 1)
                split(T_CONVOUT, 2, n, 2)
                merge(n)
            split(T_CONVOUT, 2, KD - 1, 1)

            def low_wo(k):
                dve.wait_ge(wo_hi_done, k + 1)
                dve.tensor_tensor(wo_lo[:, k, :], wo_raw[k % 4].rearrange("p k n -> p (k n)"), wo_hi[:, k, :].bitcast(F32),
                                  ALU.subtract).then_inc(wo_lo_done, 1)

            def low_of_first(b):
                dve.wait_ge(m0_hi_most, 1) if b == 0 else dve.wait_ge(m_hi_done, 2)
                ks = slice(0, KD - 1)
                ins = dve.tensor_tensor(m_lo[b][:, ks, :], m_raw[b][:, ks, :], m_hi[b][:, ks, :].bitcast(F32), ALU.subtract)
                if b == 0:
                    ins.then_inc(m0_lo_most, 1)

            def low_of_last(b):
                dve.wait_ge(m_hi_done, b + 1)
                dve.wait_ge(merged_ready, KD)
                dve.tensor_tensor(m_lo[b][:, KD - 1, :], merged[:, b * P:(b + 1) * P], m_hi[b][:, KD - 1, :].bitcast(F32),
                                  ALU.subtract).then_inc(m_lo_done, 1)

            low_wo(0)
            low_of_first(0)
            for k in range(1, 6):
                low_wo(k)
            merge(KD - 1)
            low_of_last(0)
            low_wo(6)
            low_wo(7)
            low_of_first(1)
            low_of_last(1)

            def low_m(n, b):
                dve.wait_ge(m_hi_done, n + 1)
                dve.tensor_tensor(m_lo[b][:], m_raw[b][:], m_hi[b][:].bitcast(F32), ALU.subtract).then_inc(m_lo_done, 1)

            def residual(n, b, w_, landed):
                dve.wait_ge(m_rstd, n + 1)
                if not (isinstance(n, int) and n < 2):
                    dve.wait_ge(x1_stored[b], landed - 16)
                    dve.wait_ge(x1_sq, n - 1)
                did(dve.scalar_tensor_tensor(x1[b][:].rearrange("p (a n) -> p a n", a=2), ps[:, 2 * b:2 * b + 2, :],
                                             stats[:, 8 + b:9 + b], tabs[:, R_G1 * 2 + w_, :].rearrange("p (a n) -> p a n", a=2),
                                             ALU.mult, ALU.mult))
                dve.wait_ge(xr_in[b], landed)
                settle()
                dve.tensor_tensor(x1[b][:], x1[b][:], x_res[b][:], ALU.add).then_inc(x1_ready, 1)

            def ffn_input(n, b, w_, landed):
                dve.wait_ge(x1_rstd, n + 1)
                if not (isinstance(n, int) and n < 2):
                    dve.wait_ge(h2_stored[b], landed - 16)
                    dve.wait_ge(h2_turned, n - 1)
                did(dve.scalar_tensor_tensor(h2[b][:], x1[b][:], stats[:, 12 + b:13 + b], tabs[:, R_A2 * 2 + w_, :], ALU.mult, ALU.mult))
                settle()
                dve.tensor_tensor(h2[b][:], h2[b][:], tabs[:, R_SH2 * 2 + w_, :], ALU.add).then_inc(h2_ready, 1)

            def top_logit(n):
                dve.wait_ge(logit_made, n + 1)
                did(dve.tensor_reduce(stats[:, 20:21], ps[:, 6, 0:EXPERTS], AX_X, ALU.max))
                settle()
                dve.tensor_scalar(stats[:, 10:11], stats[:, 20:21], -1.0, None, ALU.mult).then_inc(logit_max, 1)

            def affinities(n):
                a = aff_of(n)
                dve.wait_ge(logit_exp, n + 1)
                did(dve.reciprocal(stats[:, 21:22], stats[:, 11:12]))
                settle()
                dve.tensor_scalar(a, a, stats[:, 21:22], None, ALU.mult).then_inc(aff_done, 1)

            def tables(w_):
                dve.wait_ge(tabs_in[w_], 16 * (3 if w_ else 5))
                g1_, a2_ = tabs[:, R_G1 * 2 + w_, :], tabs[:, R_A2 * 2 + w_, :]
                did(dve.tensor_tensor(g1_, g1_, norm_bc[:, 0, :], ALU.mult))
                did(dve.scalar_tensor_tensor(a2_, a2_, 1.0, norm_bc[:, 1, :], ALU.add, ALU.mult))
                settle()

            def mix_step(n, b, w_, landed=None, more=True, mixed=True):
                routed = not isinstance(n, int) or n >= 3
                if routed:
                    top_logit(n - 3)
                if mixed:
                    residual(n - 1, 1 - b, w_, landed)
                if more:
                    low_m(n + 1, 1 - b)
                if routed:
                    affinities(n - 3)
                if mixed:
                    ffn_input(n - 1, 1 - b, w_, landed)

            dve.wait_ge(merged_stored, 16 * 2 * KD)
            dve.wait_ge(m_lo_done, 2)
            did(dve.memset(aff[:, :, 1, :], 0.0))
            tables(0)
            mix_step(1, 1, 0, 16)
            tables(1)
            mix_step(2, 0, 1, 16)
            with steps.loop(2, 8) as i:
                mix_step(2 * i + 3, 1, 1, 16 * (i + 2))
                mix_step(2 * i + 4, 0, 1, 16 * (i + 2))
            mix_step(7, 1, 1, 16 * 4)
            mix_step(8, 0, 1, 16 * 4, more=False)
            mix_step(9, 1, 1, 16 * 5, more=False)
            mix_step(10, 0, 1, more=False, mixed=False)
            mix_step(11, 1, 1, more=False, mixed=False)

            dve.wait_ge(aff_turned, 1)
            did(dve.tensor_copy(affT[0:EXPERTS, HALF:HALF + CTX], ps[0:EXPERTS, 1, 0:P]))
            dve.tensor_copy(affT[:, 0:HALF], ps[0:E2 + EXPERTS, 0, :]).then_inc(affT_ready, 1)
            dve.wait_ge(affT_ready, 1)
            for rows, pool_of, first, rounds in ((slice(0, EXPERTS), affT[0:EXPERTS, HALF:HALF + CTX], CAP_L, CAP_C // 8),
                                                 (slice(0, E2 + EXPERTS), affT[:, 0:HALF], 0, CAP_L // 8)):
                for r in range(rounds):
                    here = slice(first + 8 * r, first + 8 * r + 8)
                    settle()
                    did(dve.max(sel_v[rows, here], pool_of))
                    settle()
                    did(dve.max_index(sel_i[rows, here], sel_v[rows, here], pool_of))
                    settle()
                    did(dve.match_replace(pool_of, sel_v[rows, here], pool_of, -1.0))
            settle()
            dve.tensor_scalar(sel_f[:, 0:CAP_L], sel_i[:, 0:CAP_L], float(CTX), None, ALU.add).then_inc(sel_ready, 1)
            dve.tensor_copy(sel_f[0:EXPERTS, CAP_L:CAP], sel_i[0:EXPERTS, CAP_L:CAP]).then_inc(sel_ready, 1)
            dve.wait_ge(sel_turned, 1)
            dve.tensor_copy(halves[:], ps[:, 4, 0:96].rearrange("p (a e) -> p a e", a=2)).then_inc(sel_copied, 1)
            dve.tensor_copy(idx_c[:], ps[0:CAP_C, 4, 112:128]).then_inc(sel_read, 1)
            dve.tensor_copy(val_c[:], ps[0:CAP_C, 4, 96:112]).then_inc(sel_read, 1)
            a_v, a_i, spare, d = halves[:, 0, 0:EXPERTS], halves[:, 1, 0:EXPERTS], halves[:, 0, EXPERTS:E2], halves[:, 1, EXPERTS:E2]
            b_v, b_i = ps[:, 5, 0:EXPERTS], ps[:, 5, EXPERTS:2 * EXPERTS]
            dve.wait_ge(sel_copied, 1)
            dve.wait_ge(sel_flipped, 1)
            dve.tensor_tensor(val_l[:], a_v, b_v, ALU.max).then_inc(sel_read, 1)
            did(dve.tensor_tensor(spare, a_v, b_v, ALU.is_ge))
            did(dve.scalar_tensor_tensor(d, a_i, -float(HALF), b_i, ALU.add, ALU.subtract))
            settle()
            did(dve.tensor_tensor(d, d, spare, ALU.mult))
            settle()
            dve.scalar_tensor_tensor(idx_l[:], b_i, float(HALF), d, ALU.add, ALU.add).then_inc(sel_read, 1)
            dve.wait_ge(sel_read, 4)

            dve.wait_ge(g2_in, 32)
            dve.wait_ge(norm_ffn_in, 16)
            for w_ in range(2):
                dve.tensor_tensor(g2[:, w_, :], g2[:, w_, :], norm_ffn[:], ALU.mult).then_inc(g2_ready, 1)

            def expert(e):
                for q in range(4):
                    dve.wait_ge(unit_made, 12 * e + 2 * q + 2)
                    dve.wait_ge(unit_act, 8 * e + q + 1)
                    dve.tensor_tensor(hid[:, 2 * q:2 * q + 2, :],
                                      ps[:, (2 * q + 1) % 4, 0:2 * CAP].rearrange("p (m n) -> p m n", m=2), sg[:], ALU.mult)\
                       .then_inc(unit_dve, 1)
                dve.wait_ge(out_turned, e + 1)
                dve.wait_ge(added_l, 16 * e)
                dve.wait_ge(added_c, 16 * e)
                dve.tensor_scalar(ot_l[:].rearrange("p (a n) -> p a n", a=2), ps[:, 4:6, :], val_l[:, bass.ds(e, 1)], None,
                                  ALU.mult).then_inc(out_ready, 1)
                dve.tensor_scalar(ot_c[:].rearrange("p (a n) -> p a n", a=2), ps[0:CAP_C, 6:8, :], val_c[:, bass.ds(e, 1)], None,
                                  ALU.mult).then_inc(out_ready, 1)
            each(dve, EXPERTS, expert)


            dve.wait_ge(g2_ready, 2)
            dve.wait_ge(x1_landed, 16)
            for g in range(3):
                dve.wait_ge(f_in_s[g], 16)
                for t in (3 * g, 3 * g + 1):
                    did(dve.tensor_tensor(y_all[:, t, :], f_all[:, t, :], g2[:, min(t, 1), :], ALU.mult))
                settle()
                dve.wait_ge(f_rstd, g + 1)
                for t in range(3 * g, 3 * g + 3):
                    if t % 3 == 2:
                        dve.wait_ge(f_scaled, g + 1)
                    dve.scalar_tensor_tensor(y_all[:, t, :], y_all[:, t, :], f_rs[:, t:t + 1], x1_all[:, t, :], ALU.mult, ALU.add)\
                       .then_inc(y_ready, 1)


_INS = ["x_prompt", "x_sample", "state_ret_fwd", "state_ret_bwd", "c", "c_ctx", "w_ada", "b_ada", "norm_pre_mix",
        "norm_post_mix", "norm_pre_ffn", "norm_post_ffn", "w_in", "ret_decay_fwd", "ret_decay_bwd", "ret_norm_g",
        "conv_w", "w_ret_o", "w_conv_o", "w_o", "w_router", "w_gate", "w_up", "w_down"]
_OUTS = [(1, CTX, D), (1, LAT, D), (1, 1, HEADS, DK, DV), (1, 1, HEADS, DK, DV)]


def kernel(**inputs):
    import concourse.bacc as _bacc
    from concourse.bass_utils import run_bass_kernel_spmd as _run

    nc = _bacc.Bacc("TRN2", target_bir_lowering=False, num_devices=1)
    arrays, args = {}, []
    for name in _INS:
        a = np.ascontiguousarray(inputs[name])
        arrays[f"in_{name}_dram"] = a
        args.append(nc.dram_tensor(f"in_{name}_dram", a.shape, F32, kind="ExternalInput").ap())
    small, rope = shape_tables()
    for name, a in (("small", small), ("rope", rope)):
        arrays[f"table_{name}_dram"] = np.ascontiguousarray(a)
        args.append(nc.dram_tensor(f"table_{name}_dram", a.shape, F32, kind="ExternalInput").ap())
    for i, shape in enumerate(_OUTS):
        args.append(nc.dram_tensor(f"out_{i}_dram", shape, F32, kind="ExternalOutput").ap())
    build(nc, *args)
    r = _run(nc, [arrays], core_ids=[0])
    return tuple(r.results[0][f"out_{i}_dram"] for i in range(len(_OUTS)))
```
